# Optimizing a Trainium2 kernel written in Bass

```python
import math
import jax, jax.numpy as jnp
from jax import lax
import numpy as np

D_MODEL = 1024
BATCH = 1
SEQ = 256
DEPTH = 1

CONV_DIM = D_MODEL
CONV_WIDTH = 3
N_HEADS = 16
HEAD_DIM = 64
ATTN_DIM = N_HEADS * HEAD_DIM
MOBA_BLOCK = 256
TOP_BLOCKS = 3
Q_CHUNK = 32
ROPE_THETA = 10000.0
IN_PROJ_DIM = 3 * CONV_DIM + 3 * ATTN_DIM + 2 * D_MODEL
N_EXPERTS = 32
TOP_K = 4
D_FF = D_MODEL
SWIGLU_LIMIT = 7.0
SWIGLU_ALPHA = 1.702
MOE_BLOCK = 128
EPS = 1e-5

kernel_name = "hybrid_gated_conv_moba_moe_block"

def rmsnorm(x, g):
    xf = x.astype(jnp.float32)
    y = xf * lax.rsqrt(jnp.mean(xf * xf, axis=-1, keepdims=True) + EPS)
    return (y * g.astype(jnp.float32)).astype(x.dtype)

def rope(t, positions):
    half = HEAD_DIM // 2
    inv_freq = ROPE_THETA ** (-jnp.arange(0, half, dtype=jnp.float32) / half)
    ang = positions.astype(jnp.float32)[:, None] * inv_freq[None, :]
    cos = jnp.cos(ang)[None, None]
    sin = jnp.sin(ang)[None, None]
    tf = t.astype(jnp.float32)
    t1, t2 = tf[..., :half], tf[..., half:]
    out = jnp.concatenate([t1 * cos - t2 * sin, t2 * cos + t1 * sin], axis=-1)
    return out.astype(t.dtype)

def short_conv(u, conv_w):
    rhs = conv_w[:, None, :]
    return lax.conv_general_dilated(
        u, rhs, window_strides=(1,), padding=[(CONV_WIDTH - 1, 0)],
        dimension_numbers=("NWC", "WIO", "NWC"), feature_group_count=u.shape[-1])

def moba_attention(q, k, v):
    b, h, s, dh = q.shape
    s_pad = ((s + MOBA_BLOCK - 1) // MOBA_BLOCK) * MOBA_BLOCK
    pad = s_pad - s
    if pad:
        cfg = ((0, 0), (0, 0), (0, pad), (0, 0))
        q, k, v = jnp.pad(q, cfg), jnp.pad(k, cfg), jnp.pad(v, cfg)
    nb = s_pad // MOBA_BLOCK
    n_top = min(TOP_BLOCKS, nb)
    k_blocks = k.reshape(b, h, nb, MOBA_BLOCK, dh)
    v_blocks = v.reshape(b, h, nb, MOBA_BLOCK, dh)
    k_mean = jnp.mean(k_blocks.astype(jnp.float32), axis=3)
    scale = HEAD_DIM ** -0.5
    block_ids = jnp.arange(nb)
    key_offsets = jnp.arange(MOBA_BLOCK)
    gather_blocks = jax.vmap(jax.vmap(lambda kb, idx: kb[idx]))

    def chunk(c):
        start = c * Q_CHUNK
        own = start // MOBA_BLOCK
        q_c = lax.dynamic_slice_in_dim(q, start, Q_CHUNK, axis=2)
        q_pos = start + jnp.arange(Q_CHUNK)
        gate = jnp.einsum("bhqd,bhnd->bhqn", q_c.astype(jnp.float32), k_mean)
        gate = jnp.where((block_ids < own)[None, None, None, :], gate, -jnp.inf)
        g_val, sel = lax.top_k(gate, n_top)
        sel_valid = jnp.isfinite(g_val)
        k_sel = gather_blocks(k_blocks, sel)
        v_sel = gather_blocks(v_blocks, sel)
        s_sel = jnp.einsum("bhqd,bhqtkd->bhqtk", q_c, k_sel).astype(jnp.float32) * scale
        s_sel = jnp.where(sel_valid[..., None], s_sel, -jnp.inf)
        s_sel = s_sel.reshape(b, h, Q_CHUNK, n_top * MOBA_BLOCK)
        k_own = lax.dynamic_slice_in_dim(k, own * MOBA_BLOCK, MOBA_BLOCK, axis=2)
        v_own = lax.dynamic_slice_in_dim(v, own * MOBA_BLOCK, MOBA_BLOCK, axis=2)
        s_own = jnp.einsum("bhqd,bhkd->bhqk", q_c, k_own).astype(jnp.float32) * scale
        causal = (own * MOBA_BLOCK + key_offsets)[None, :] <= q_pos[:, None]
        s_own = jnp.where(causal[None, None], s_own, -jnp.inf)
        p = jax.nn.softmax(jnp.concatenate([s_sel, s_own], axis=-1), axis=-1).astype(v.dtype)
        p_sel = p[..., : n_top * MOBA_BLOCK].reshape(b, h, Q_CHUNK, n_top, MOBA_BLOCK)
        p_own = p[..., n_top * MOBA_BLOCK:]
        return (jnp.einsum("bhqtk,bhqtkd->bhqd", p_sel, v_sel)
                + jnp.einsum("bhqk,bhkd->bhqd", p_own, v_own))

    outs = lax.map(chunk, jnp.arange(s_pad // Q_CHUNK))
    out = outs.transpose(1, 2, 0, 3, 4).reshape(b, h, s_pad, dh)
    return out[:, :, :s]

def moe(hn, router_w, router_b, w_gate_up, b_gate_up, w_down, b_down):
    n, d = hn.shape
    logits = (hn @ router_w + router_b).astype(jnp.float32)
    top_val, top_idx = lax.top_k(logits, TOP_K)
    top_w = jax.nn.softmax(top_val, axis=-1).astype(hn.dtype)
    nk = n * TOP_K
    flat_e = top_idx.reshape(nk)
    flat_tok = jnp.repeat(jnp.arange(n, dtype=jnp.int32), TOP_K)
    flat_w = top_w.reshape(nk)
    order = jnp.argsort(flat_e, stable=True)
    sorted_e = flat_e[order]
    counts = jnp.bincount(flat_e, length=N_EXPERTS)
    padded_counts = ((counts + MOE_BLOCK - 1) // MOE_BLOCK) * MOE_BLOCK
    start_sorted = jnp.cumsum(counts) - counts
    padded_end = jnp.cumsum(padded_counts)
    start_pad = padded_end - padded_counts
    rank = jnp.arange(nk) - start_sorted[sorted_e]
    dest = start_pad[sorted_e] + rank
    n_slots = ((nk + N_EXPERTS * (MOE_BLOCK - 1) + MOE_BLOCK - 1) // MOE_BLOCK) * MOE_BLOCK
    n_blocks = n_slots // MOE_BLOCK
    slot_tok = jnp.full((n_slots,), n, dtype=jnp.int32).at[dest].set(flat_tok[order])
    slot_w = jnp.zeros((n_slots,), hn.dtype).at[dest].set(flat_w[order])
    block_expert = jnp.clip(
        jnp.searchsorted(padded_end, jnp.arange(n_blocks) * MOE_BLOCK, side="right"),
        0, N_EXPERTS - 1)
    h_ext = jnp.concatenate([hn, jnp.zeros((1, d), hn.dtype)], axis=0)
    xs = h_ext[slot_tok].reshape(n_blocks, MOE_BLOCK, d)

    def expert_block(args):
        xb, e = args
        gu = xb @ w_gate_up[e] + b_gate_up[e]
        gate = jnp.minimum(gu[:, :D_FF], SWIGLU_LIMIT)
        up = jnp.clip(gu[:, D_FF:], -SWIGLU_LIMIT, SWIGLU_LIMIT)
        act = (up + 1.0) * (gate * jax.nn.sigmoid(SWIGLU_ALPHA * gate))
        return act @ w_down[e] + b_down[e]

    ys = lax.map(expert_block, (xs, block_expert)).reshape(n_slots, d) * slot_w[:, None]
    out = jnp.zeros((n + 1, d), hn.dtype).at[slot_tok].add(ys)
    return out[:n]

def setup_inputs(seed: int = 0) -> dict:
    key = jax.random.key(seed)
    ks = jax.random.split(key, 16)
    f32 = jnp.float32
    nrm = lambda k, shape, fan_in: jax.random.normal(k, shape, f32) * (fan_in ** -0.5)
    return {
        "x": jax.random.normal(ks[0], (BATCH, SEQ, D_MODEL), f32),
        "norm_mix_g": 1.0 + 0.02 * jax.random.normal(ks[1], (D_MODEL,), f32),
        "w_in": nrm(ks[2], (D_MODEL, IN_PROJ_DIM), D_MODEL),
        "conv_w": nrm(ks[3], (CONV_WIDTH, CONV_DIM), CONV_WIDTH),
        "w_conv_out": nrm(ks[4], (CONV_DIM, D_MODEL), CONV_DIM),
        "w_attn_out": nrm(ks[5], (ATTN_DIM, D_MODEL), ATTN_DIM),
        "w_out": nrm(ks[6], (D_MODEL, D_MODEL), D_MODEL),
        "norm_ffn_g": 1.0 + 0.02 * jax.random.normal(ks[7], (D_MODEL,), f32),
        "router_w": nrm(ks[8], (D_MODEL, N_EXPERTS), D_MODEL),
        "router_b": 0.01 * jax.random.normal(ks[9], (N_EXPERTS,), f32),
        "w_gate_up": nrm(ks[10], (N_EXPERTS, D_MODEL, 2 * D_FF), D_MODEL),
        "b_gate_up": 0.02 * jax.random.normal(ks[11], (N_EXPERTS, 2 * D_FF), f32),
        "w_down": nrm(ks[12], (N_EXPERTS, D_FF, D_MODEL), D_FF),
        "b_down": 0.02 * jax.random.normal(ks[13], (N_EXPERTS, D_MODEL), f32),
        "norm_final_g": 1.0 + 0.02 * jax.random.normal(ks[14], (D_MODEL,), f32),
    }

def reference(x, norm_mix_g, w_in, conv_w, w_conv_out, w_attn_out, w_out, norm_ffn_g,
              router_w, router_b, w_gate_up, b_gate_up, w_down, b_down, norm_final_g):
    b, s, d = x.shape
    positions = jnp.arange(s, dtype=jnp.int32)
    h = x
    for _ in range(DEPTH):
        xn = rmsnorm(h, norm_mix_g)
        z = xn @ w_in
        splits = np.cumsum([CONV_DIM, CONV_DIM, CONV_DIM, ATTN_DIM, ATTN_DIM, ATTN_DIM, D_MODEL]).tolist()
        c_b, c_c, c_x, q, k, v, g_conv, g_attn = jnp.split(z, splits, axis=-1)
        y_conv = (c_b * short_conv(c_c * c_x, conv_w)) @ w_conv_out
        to_heads = lambda t: t.reshape(b, s, N_HEADS, HEAD_DIM).transpose(0, 2, 1, 3)
        qh = rope(to_heads(q), positions)
        kh = rope(to_heads(k), positions)
        vh = to_heads(v)
        attn = moba_attention(qh, kh, vh).transpose(0, 2, 1, 3).reshape(b, s, ATTN_DIM)
        y_attn = attn @ w_attn_out
        merged = jax.nn.sigmoid(g_conv) * y_conv + jax.nn.sigmoid(g_attn) * y_attn
        h = h + merged @ w_out
        hn = rmsnorm(h, norm_ffn_g).reshape(b * s, d)
        h = h + moe(hn, router_w, router_b, w_gate_up, b_gate_up, w_down, b_down).reshape(b, s, d)
    return rmsnorm(h, norm_final_g)


_drawn_inputs = setup_inputs


def setup_inputs(seed=0):
    import zlib

    import numpy as np

    out = dict(_drawn_inputs(seed))
    spreads = {}
    factors = {'b_gate_up': 5.658, 'b_down': 6.434, 'norm_final_g': 2.879}
    for name, (base, spread) in spreads.items():
        noise = np.random.default_rng([zlib.crc32(name.encode()), seed]).standard_normal(out[name].shape)
        drawn = base * np.exp(spread * noise) if base else spread * noise
        out[name] = __import__('jax').numpy.asarray(drawn.astype(out[name].dtype))
    for name, factor in factors.items():
        out[name] = (out[name] * factor).astype(out[name].dtype)
    return out
```

```python
from contextlib import ExitStack

import numpy as np

import concourse.bass as bass
from concourse import mybir

F32 = mybir.dt.float32
I32 = mybir.dt.int32
ALU = mybir.AluOpType
ACT = mybir.ActivationFunctionType
AX_X = mybir.AxisListType.X

P = 128
D = 1024
SEQ = 256
HEADS = 16
HEAD_DIM = 64
EXPERTS = 32
TOP_K = 4
D_FF = 1024
EPS = 1e-5
SWIGLU_LIMIT = 7.0
SWIGLU_ALPHA = 1.702
ROPE_THETA = 10000.0
SCALE = HEAD_DIM ** -0.5

KC = D // P
TT = SEQ // P
HALF = 512
PAIRS = HEADS // 2
COLS = 256
UNIT = KC * COLS
RING = 12
SLOTS = 64
FIRST_SLOT = 0
PASSES = (FIRST_SLOT + SEQ + SLOTS - 1) // SLOTS
MASKED = -3.0e38
ROUTE_STEPS = 3

GROUPS = [("q", 3 * D), ("k", 4 * D), ("v", 5 * D), ("conv_c", D), ("conv_x", 2 * D), ("conv_b", 0),
          ("gate_conv", 6 * D), ("gate_attn", 7 * D)]
PER_GROUP = D // COLS
IN_UNITS = [(g, i, c0 + i * COLS) for g, c0 in GROUPS for i in range(PER_GROUP)]
OUT_UNITS = [(g, i, i * COLS) for g in ("conv_out", "attn_out", "w_out") for i in range(PER_GROUP)]
MIX_UNITS = IN_UNITS + OUT_UNITS
N_MIX = len(MIX_UNITS)
ATTN_FROM = 3 * PER_GROUP
GU_UNITS = KC
DOWN_UNITS = KC // 2
EXPERT_UNITS = GU_UNITS + DOWN_UNITS
assert EXPERT_UNITS == RING
BY_ACT = ("q", "k", "v", "conv_c", "gate_conv", "gate_attn")

TABLE = {}
_at = 0
for _name, _n in (("ident", P), ("before", P), ("ones", P), ("causal", P), ("cos", SEQ), ("sin", SEQ),
                  ("slot", 2 * SLOTS), ("rank", EXPERTS)):
    TABLE[_name] = (_at, _at + _n)
    _at += _n
TABLE_COLS = _at


def constants():
    t = np.zeros((P, TABLE_COLS), np.float32)

    def put(name, a):
        lo, hi = TABLE[name]
        t[:, lo:hi] = a

    i = np.arange(P)
    put("ident", np.eye(P))
    put("before", i[:, None] < i[None, :])
    put("ones", 1.0)
    put("causal", np.where(i[None, :] <= i[:, None], 0.0, MASKED))
    half = HEAD_DIM // 2
    inv_freq = np.float32(ROPE_THETA) ** (-np.arange(half, dtype=np.float32) / np.float32(half))
    ang = np.arange(SEQ, dtype=np.float32)[None, :] * inv_freq.astype(np.float32)[i % half][:, None]
    put("cos", np.cos(ang))
    put("sin", np.where((i % HEAD_DIM < half)[:, None], -np.sin(ang), np.sin(ang)))
    put("slot", np.arange(2 * SLOTS) % SLOTS)
    put("rank", EXPERTS - np.arange(EXPERTS))
    return t


def build(nc, x, table, norm_mix_g, w_in, conv_w, w_conv_out, w_attn_out, w_out, norm_ffn_g, router_w,
          router_b, w_gate_up, b_gate_up, w_down, b_down, norm_final_g, out):
    with ExitStack() as ctx:
        def sb(name, shape, dt=F32):
            return ctx.enter_context(nc.sbuf_tensor(name, shape, dt))

        def sem(name):
            return ctx.enter_context(nc.semaphore(name))

        ring = sb("ring", [P, RING, UNIT])
        tab = sb("tab", [P, TABLE_COLS])
        h_tok = sb("h_tok", [P, TT, D])
        n_tok = sb("n_tok", [P, TT, D])
        n_feat = sb("n_feat", [P, KC, SEQ])
        q_feat = sb("q_feat", [P, PAIRS, SEQ])
        area_a = sb("area_a", [P, 2 * KC * SEQ])
        area_b = sb("area_b", [P, KC * SEQ])
        area_c = sb("area_c", [P, KC, SEQ + 2])
        z_raw = sb("z_raw", [P, 2, SEQ])
        z_swap = sb("z_swap", [P, 2, SEQ])
        prob = sb("prob", [P, 2, 3 * P])
        prob_t = sb("prob_t", [P, 2, 3 * P])
        b_gu = sb("b_gu", [P, 2 * D_FF])
        b_dn = sb("b_dn", [EXPERTS, D])
        g_ffn = sb("g_ffn", [P, D])
        g_fin = sb("g_fin", [P, D])
        g_mix = sb("g_mix", [P, KC])
        taps = sb("taps", [P, KC, 3])
        r_w = sb("r_w", [P, KC, EXPERTS])
        r_b = sb("r_b", [EXPERTS, 1])
        stat = sb("stat", [P, 8])
        neg_max = sb("neg_max", [P, 4])
        row_max = sb("row_max", [P, 4])
        row_sum = sb("row_sum", [P, 4])
        row_inv = sb("row_inv", [P, 4])
        logit_f = sb("logit_f", [EXPERTS, SEQ])
        logit = sb("logit", [P, TT, EXPERTS])
        left = sb("left", [P, TT, EXPERTS])
        hit = sb("hit", [P, TT, EXPERTS])
        top = sb("top", [P, TT])
        top0 = sb("top0", [P, TT])
        first = sb("first", [P, TT])
        chosen = sb("chosen", [P, TT, EXPERTS])
        weight = sb("weight", [P, TT, EXPERTS])
        weight_t = sb("weight_t", [EXPERTS, SEQ])
        slot_of = sb("slot_of", [P, TT, EXPERTS + 1])
        most = sb("most", [P, 1])
        most_i = sb("most_i", [P, 1], I32)
        pick = sb("pick", [P, SLOTS])

        def tb(name, lo=0, n=None):
            a, b = TABLE[name]
            return tab[:, a + lo:(b if n is None else a + lo + n)]

        k_feat = area_a[:, :].rearrange("p (j h s) -> p j h s", j=PAIRS, h=2)
        gates = area_a[:, :].rearrange("p (g c s) -> p g c s", g=2, c=KC)
        conv = area_b[:, :].rearrange("p (c s) -> p c s", c=KC)
        merged = area_c[:, :, :].rearrange("p c s -> p (c s)")[:, 0:KC * SEQ].rearrange("p (c s) -> p c s", c=KC)
        conv_tmp = z_raw
        square = area_a[:, 0:D]

        def part(area, at, n):
            return area[:, at:at + n]

        gate_sb = part(area_a, 0, HALF)
        up_sb = part(area_a, HALF, HALF)
        sig_sb = part(area_a, 2 * HALF, HALF)
        act_sb = part(area_a, 3 * HALF, HALF)
        y_sb = part(area_a, 4 * HALF, 2 * HALF).rearrange("p (n c) -> p n c", n=2)
        scat_sb = part(area_a, 6 * HALF, SEQ).rearrange("p (t c) -> p t c", t=TT)
        act_t = part(area_b, 0, HALF).rearrange("p (c s) -> p c s", c=4)
        xg_sb = part(area_b, HALF, HALF)
        xg_t = part(area_b, 2 * HALF, HALF).rearrange("p (c s) -> p c s", c=4)
        onehot = part(area_b, 3 * HALF, TT * SLOTS).rearrange("p (t s) -> p t s", t=TT)
        whot = part(area_b, 3 * HALF + TT * SLOTS, TT * P).rearrange("p (t s) -> p t s", t=TT)

        ps = ctx.enter_context(nc.psum_tensor("ps", [P, 8, HALF], F32))
        GATE, UP, Y0, Y1 = 0, 1, 2, 3
        ACT_T, SCAT_T, XG, XG_T = GATE, UP, Y0, Y1

        table_in = sem("table_in")
        x_in = sem("x_in")
        gain_in = sem("gain_in")
        small_in = sem("small_in")
        bias_in = sem("bias_in")
        slot_in = [sem(f"slot_in{i}") for i in range(RING)]
        unit_used = sem("unit_used")
        taken_act = sem("taken_act")
        taken_dve = sem("taken_dve")
        zeroed = sem("zeroed")
        bias_zeroed = sem("bias_zeroed")
        squared = sem("squared")
        meaned = sem("meaned")
        rooted = sem("rooted")
        normed = sem("normed")
        flipped = sem("flipped")
        feat_ready = sem("feat_ready")
        roped = sem("roped")
        scored = sem("scored")
        max_ready = sem("max_ready")
        exp_done = sem("exp_done")
        prob_ready = sem("prob_ready")
        prob_flipped = sem("prob_flipped")
        prob_t_ready = sem("prob_t_ready")
        attended = sem("attended")
        attn_taken = sem("attn_taken")
        routed = sem("routed")
        logit_step = sem("logit_step")
        route_step = sem("route_step")
        dve_done = sem("dve_done")
        act_done = sem("act_done")
        onehot_ready = sem("onehot_ready")
        pick_ready = sem("pick_ready")
        whot_ready = sem("whot_ready")
        gathered = sem("gathered")
        xg_ready = sem("xg_ready")
        xg_flipped = sem("xg_flipped")
        xg_t_ready = sem("xg_t_ready")
        gate_ready = sem("gate_ready")
        up_ready = sem("up_ready")
        sig_ready = sem("sig_ready")
        act_ready = sem("act_ready")
        act_flipped = sem("act_flipped")
        act_t_ready = sem("act_t_ready")
        scat_flipped = sem("scat_flipped")
        scat_ready = sem("scat_ready")
        y0_ready = sem("y0_ready")
        y1_ready = sem("y1_ready")
        scattered = sem("scattered")
        final_ready = sem("final_ready")
        stored = sem("stored")

        block = ctx.enter_context(nc.Block())

        def wait_unit(eng, n):
            eng.wait_ge(slot_in[n % RING], 16 * (n // RING + 1))

        def expert_slot(u):
            return (N_MIX + u) % RING

        def wait_expert_unit(eng, it, u):
            eng.wait_ge(slot_in[expert_slot(u)], (it + ((N_MIX + u) // RING + 1)) * 16)

        def taken(n):
            by_act = MIX_UNITS[n][0] in BY_ACT
            count = sum((m[0] in BY_ACT) == by_act for m in MIX_UNITS[:n + 1])
            return (taken_act if by_act else taken_dve), count

        def expert_passes(eng, start, body, finish):
            start(0)
            with eng.Fori(0, EXPERTS) as e:
                body(0, e)
            finish(0)
            eng.wait_ge(route_step, ROUTE_STEPS)
            count = eng.value_load(most_i[0:1, 0:1], min_val=0, max_val=2 * SEQ)
            with eng.If(count > SLOTS):
                with eng.Fori(1, PASSES) as r:
                    start(r)
                    with eng.Fori(0, EXPERTS) as e:
                        body(r, e)
                    finish(r)

        def nothing(r):
            pass

        @block.sync
        def _(sp):
            mix_dram = {"conv_out": w_conv_out, "attn_out": w_attn_out, "w_out": w_out}

            def load_unit(n):
                name, _, c0 = MIX_UNITS[n]
                src = mix_dram.get(name, w_in)[:, c0:c0 + COLS].rearrange("(k p) n -> p k n", p=P)
                if n >= RING:
                    sp.wait_ge(unit_used, n - RING + 1)
                sp.dma_start(ring[:, n % RING, :].rearrange("p (k n) -> p k n", k=KC), src).then_inc(
                    slot_in[n % RING], 16)

            sp.dma_start(h_tok[:], x.rearrange("(t p) d -> p t d", p=P)).then_inc(x_in, 16)
            sp.dma_start(tab[:], table).then_inc(table_in, 16)
            sp.dma_start(g_mix[:], norm_mix_g).then_inc(gain_in, 16)
            load_unit(0)
            load_unit(1)
            sp.dma_start(taps[:], conv_w).then_inc(small_in, 16)
            sp.dma_start(r_w[:], router_w.rearrange("(k p) e -> p k e", p=P)).then_inc(small_in, 16)
            sp.dma_start(r_b[:], router_b).then_inc(small_in, 16)
            sp.dma_start(g_ffn[:], norm_ffn_g.partition_broadcast(P)).then_inc(small_in, 16)
            sp.dma_start(g_fin[:], norm_final_g.partition_broadcast(P)).then_inc(small_in, 16)
            sp.dma_start(b_dn[:], b_down).then_inc(small_in, 16)
            sp.wait_ge(bias_zeroed, 1)
            sp.dma_start(b_gu[0:EXPERTS, :], b_gate_up).then_inc(bias_in, 16)
            for n in range(2, N_MIX):
                load_unit(n)

            def body(r, e):
                it = r * EXPERTS + e
                for u in range(EXPERT_UNITS):
                    if u < GU_UNITS:
                        src = w_gate_up[bass.ds(e, 1), u * P:(u + 1) * P, :].rearrange("e p n -> (e p) n")
                        dst = ring[:, expert_slot(u), :]
                    else:
                        j = u - GU_UNITS
                        src = w_down[bass.ds(e, 1), :, :].rearrange(
                            "e (h c p) n -> c p (e h) n", h=2, c=DOWN_UNITS)[j]
                        dst = ring[:, expert_slot(u), :].rearrange("p (h n) -> p h n", h=2)
                    sp.wait_ge(unit_used, it * EXPERT_UNITS + (N_MIX + u - RING + 1))
                    sp.dma_start(dst, src).then_inc(slot_in[expert_slot(u)], 16)

            expert_passes(sp, nothing, body, nothing)
            for t in range(TT):
                sp.wait_ge(final_ready, t + 1)
                sp.dma_start(out[t * P:(t + 1) * P, :], n_tok[:, t, :]).then_inc(stored, 16)
            sp.wait_ge(stored, 16 * TT)

        @block.gpsimd
        def _(pool):
            pool.memset(b_gu[:], 0.0).then_inc(bias_zeroed, 1)
            pool.memset(area_c[:, :, 0:2], 0.0).then_inc(zeroed, 1)
            pool.wait_ge(squared, TT)
            pool.memset(area_a[:], 0.0).then_inc(zeroed, 1)

        @block.tensor
        def _(pe):
            def flip_norm():
                for c in range(KC):
                    for t in range(TT):
                        at = (c % 2) * SEQ + t * P
                        mm = pe.transpose(ps[:, 2 + c // 2, at:at + P], n_tok[:, t, c * P:(c + 1) * P], tb("ident"))
                mm.then_inc(flipped, 1)

            def project(n):
                name, i, _ = MIX_UNITS[n]
                bank = n % 2
                w = ring[:, n % RING, :].rearrange("p (k n) -> p k n", k=KC)
                src = {"conv_out": conv, "attn_out": q_feat, "w_out": merged}.get(name, n_feat)
                wait_unit(pe, n)
                if n >= 2:
                    pe.wait_ge(*taken(n - 2))
                for m in range(2):
                    for k in range(KC):
                        if name in ("v", "w_out"):
                            left_op, right_op = src[:, k, m * P:(m + 1) * P], w[:, k, :]
                        else:
                            left_op, right_op = w[:, k, m * P:(m + 1) * P], src[:, k, :]
                        mm = pe.matmul(ps[:, bank, m * COLS:(m + 1) * COLS], left_op, right_op,
                                       start=(k == 0), stop=(k == KC - 1))
                mm.then_inc(unit_used, 1)

            def score(j):
                pe.wait_ge(roped, PER_GROUP + j // 2 + 1)
                if j >= 1:
                    pe.wait_ge(exp_done, j)
                for h in range(2):
                    pe.matmul(ps[:, 2 + h, 0:P], q_feat[:, j, 0:P], k_feat[:, j, h, 0:P], start=True, stop=True)
                    mm = pe.matmul(ps[:, 2 + h, P:3 * P], q_feat[:, j, P:SEQ], k_feat[:, j, h, :],
                                   start=True, stop=True)
                mm.then_inc(scored, 1)

            def flip_prob(j):
                pe.wait_ge(prob_ready, j + 1)
                if j >= 1:
                    pe.wait_ge(prob_t_ready, j)
                for h in range(2):
                    for b in range(3):
                        mm = pe.transpose(ps[:, 4 + h, b * P:(b + 1) * P], prob[:, h, b * P:(b + 1) * P],
                                          tb("ident"))
                mm.then_inc(prob_flipped, 1)

            def attend(j):
                pe.wait_ge(prob_t_ready, j + 1)
                if j == 0:
                    pe.wait_ge(*taken(ATTN_FROM - 1))
                else:
                    pe.wait_ge(attn_taken, j)
                for kt in range(2):
                    for h in range(2):
                        v = n_tok[:, kt, j * P + h * HEAD_DIM:j * P + (h + 1) * HEAD_DIM]
                        lo = kt * P
                        mm = pe.matmul(ps[h * HEAD_DIM:(h + 1) * HEAD_DIM, 6, lo:SEQ], v,
                                       prob_t[:, h, 2 * lo:2 * lo + SEQ - lo], start=(kt == 0), stop=(kt == 1),
                                       skip_group_check=True)
                mm.then_inc(attended, 1)

            pe.wait_ge(table_in, 16)
            pe.wait_ge(normed, 1)
            flip_norm()
            pe.wait_ge(feat_ready, 1)
            for n in range(N_MIX):
                if MIX_UNITS[n][0] == "attn_out" and MIX_UNITS[n][1] == 0:
                    pe.wait_ge(attn_taken, PAIRS)
                if MIX_UNITS[n][0] == "conv_out" and MIX_UNITS[n][1] == 0:
                    pe.wait_ge(*taken(6 * PER_GROUP - 1))
                if MIX_UNITS[n][0] == "w_out" and MIX_UNITS[n][1] == 0:
                    pe.wait_ge(*taken(n - 1))
                project(n)
                s = n - ATTN_FROM
                if 0 <= s < PAIRS:
                    score(s)
                if 1 <= s < PAIRS + 1:
                    flip_prob(s - 1)
                if 2 <= s < PAIRS + 2:
                    attend(s - 2)

            pe.wait_ge(normed, 2)
            flip_norm()
            pe.wait_ge(feat_ready, 2)
            pe.wait_ge(small_in, 16 * 6)
            for k in range(KC):
                mm = pe.matmul(ps[0:EXPERTS, 0, 0:SEQ], r_w[:, k, :], n_feat[:, k, :], start=(k == 0),
                               stop=(k == KC - 1))
            mm.then_inc(routed, 1)
            pe.wait_ge(logit_step, 1)
            for t in range(TT):
                mm = pe.transpose(ps[:, 1, t * EXPERTS:(t + 1) * EXPERTS], logit_f[:, t * P:(t + 1) * P],
                                  tb("ident")[0:EXPERTS, 0:EXPERTS])
            mm.then_inc(routed, 1)
            pe.wait_ge(route_step, 1)
            pe.matmul(ps[:, 2, 0:EXPERTS], tb("before"), chosen[:, 0, :], start=True, stop=True)
            for lo, first_op in ((1, "before"), (2, "ones")):
                pe.matmul(ps[:, 2, lo * EXPERTS:(lo + 1) * EXPERTS], tb("ones"), chosen[:, 0, :],
                          start=True, stop=False)
                mm = pe.matmul(ps[:, 2, lo * EXPERTS:(lo + 1) * EXPERTS], tb(first_op), chosen[:, 1, :],
                               start=False, stop=True)
            mm.then_inc(routed, 1)
            pe.wait_ge(route_step, 2)
            for t in range(TT):
                mm = pe.transpose(ps[0:EXPERTS, 3, t * P:(t + 1) * P], weight[:, t, :], tb("ident"))
            mm.then_inc(routed, 1)
            pe.wait_ge(logit_step, 3)
            for t in range(TT):
                for n in range(2):
                    mm = pe.matmul(ps[:, 4 + 2 * t + n, :], weight_t[:, t * P:(t + 1) * P],
                                   b_dn[:, n * HALF:(n + 1) * HALF], start=True, stop=True)
            mm.then_inc(scat_flipped, 1)

            def gather(g, busy):
                pe.wait_ge(onehot_ready, g)
                pe.wait_ge(y0_ready, busy)
                for t in range(TT):
                    for n in range(2):
                        mm = pe.matmul(ps[n * SLOTS:(n + 1) * SLOTS, XG, :], onehot[:, t, :],
                                       n_tok[:, t, n * HALF:(n + 1) * HALF], start=(t == 0), stop=(t == TT - 1),
                                       skip_group_check=True)
                mm.then_inc(gathered, 1)

            def flip_gathered(g, busy):
                pe.wait_ge(xg_ready, g)
                pe.wait_ge(y1_ready, busy)
                for c in range(4):
                    mm = pe.transpose(ps[:, XG_T, c * P:(c + 1) * P], xg_sb[:, c * P:(c + 1) * P], tb("ident"))
                mm.then_inc(xg_flipped, 1)

            def scatter():
                for t in range(TT):
                    for n in range(2):
                        mm = pe.matmul(ps[:, 4 + 2 * t + n, :], scat_sb[:, t, :], y_sb[:, n, :],
                                       start=False, stop=True, skip_group_check=True)
                return mm

            def start(r):
                g = r * (EXPERTS + 1) + 1
                gather(g, r * EXPERTS + 1)
                flip_gathered(g, r * EXPERTS + 1)

            def body(r, e):
                it = r * EXPERTS + e
                g = r * (EXPERTS + 1) + e + 1
                pe.wait_ge(pick_ready, g)
                pe.wait_ge(act_t_ready, it + 1)
                pe.wait_ge(scat_ready, it + 1)
                for b in range(2):
                    for h in range(2):
                        lo = b * D_FF + h * HALF
                        pe.matmul(ps[h * SLOTS:(h + 1) * SLOTS, GATE + b, :], pick[:], b_gu[:, lo:lo + HALF],
                                  start=True, stop=False, skip_group_check=True)
                pe.wait_ge(xg_t_ready, g)
                for k in range(GU_UNITS):
                    wait_expert_unit(pe, it, k)
                    for b in range(2):
                        for h in range(2):
                            lo = b * D_FF + h * HALF
                            mm = pe.matmul(ps[h * SLOTS:(h + 1) * SLOTS, GATE + b, :],
                                           xg_t[:, k % 4, (k // 4) * SLOTS:(k // 4 + 1) * SLOTS],
                                           ring[:, expert_slot(k), lo:lo + HALF],
                                           start=False, stop=(k == GU_UNITS - 1), skip_group_check=True)
                    mm.then_inc(unit_used, 1)
                gather(g + 1, it + 1)
                scatter_waits(it + 1)
                scatter()
                flip_gathered(g + 1, it + 1)
                pe.wait_ge(act_ready, it + 1)
                for c in range(4):
                    mm = pe.transpose(ps[:, ACT_T, c * P:(c + 1) * P], act_sb[:, c * P:(c + 1) * P], tb("ident"))
                mm.then_inc(act_flipped, 1)
                pe.wait_ge(whot_ready, it + 1)
                for t in range(TT):
                    mm = pe.transpose(ps[:, SCAT_T, t * P:(t + 1) * P], whot[:, t, :], tb("ident"))
                mm.then_inc(scat_flipped, 1)
                pe.wait_ge(act_t_ready, it + 2)
                pe.wait_ge(xg_t_ready, g + 1)
                for j in range(DOWN_UNITS):
                    wait_expert_unit(pe, it, GU_UNITS + j)
                    for n in range(2):
                        for h in range(2):
                            lo = h * D + n * HALF
                            mm = pe.matmul(ps[h * SLOTS:(h + 1) * SLOTS, Y0 + n, :],
                                           act_t[:, j, h * SLOTS:(h + 1) * SLOTS],
                                           ring[:, expert_slot(GU_UNITS + j), lo:lo + HALF],
                                           start=(j == 0), stop=(j == DOWN_UNITS - 1), skip_group_check=True)
                    mm.then_inc(unit_used, 1)

            def scatter_waits(n):
                pe.wait_ge(y0_ready, n)
                pe.wait_ge(y1_ready, n)
                pe.wait_ge(scat_ready, n)

            def finish(r):
                scatter_waits((r + 1) * EXPERTS + 1)
                scatter().then_inc(scattered, 1)

            expert_passes(pe, start, body, finish)

        @block.scalar
        def _(act):
            chain = [0]

            def squares(n):
                for t in range(TT):
                    if n or t:
                        act.wait_ge(squared, n * TT + t)
                    act.activation(square, h_tok[:, t, :], ACT.Square,
                                   accum_out=stat[:, t:t + 1]).then_inc(squared, 1)

            def root(n):
                act.wait_ge(meaned, n)
                act.activation(stat[:, 4:4 + TT], stat[:, 2:2 + TT], ACT.Sqrt).then_inc(rooted, 1)

            def take(n):
                name, i, _ = MIX_UNITS[n]
                act.wait_ge(unit_used, n + 1)
                src = ps[:, n % 2, :].rearrange("p (m s) -> p m s", m=2)
                if name in ("q", "k"):
                    if n >= 1:
                        act.wait_ge(roped, n)
                    act.copy(z_raw[:], src)
                    for a in range(4):
                        b = a ^ 1
                        last = act.copy(z_swap[32 * a:32 * a + 32, :, :], src[32 * b:32 * b + 32, :, :])
                    last.then_inc(taken_act, 1)
                elif name == "v":
                    act.copy(n_tok[:, :, i * COLS:(i + 1) * COLS], src).then_inc(taken_act, 1)
                elif name == "conv_c":
                    act.copy(conv[:, 2 * i:2 * i + 2, :], src).then_inc(taken_act, 1)
                else:
                    g = ("gate_conv", "gate_attn").index(name)
                    act.activation(gates[:, g, 2 * i:2 * i + 2, :], src, ACT.Sigmoid).then_inc(taken_act, 1)

            def exps(j):
                act.wait_ge(max_ready, j + 1)
                if j >= 1:
                    act.wait_ge(prob_flipped, j)
                for h in range(2):
                    for q in range(2):
                        i = 2 * h + q
                        lo, hi = (0, P) if q == 0 else (P, 3 * P)
                        last = act.activation(prob[:, h, lo:hi], ps[:, 2 + h, lo:hi], ACT.Exp,
                                              bias=neg_max[:, i:i + 1], scale=SCALE,
                                              accum_out=row_sum[:, i:i + 1])
                last.then_inc(exp_done, 1)

            def take_prob_t(j):
                act.wait_ge(prob_flipped, j + 1)
                if j >= 1:
                    act.wait_ge(attended, j)
                act.copy(prob_t[:], ps[:, 4:6, 0:3 * P]).then_inc(prob_t_ready, 1)

            act.wait_ge(x_in, 16)
            squares(0)
            root(1)
            for n in range(N_MIX):
                if MIX_UNITS[n][0] in BY_ACT:
                    take(n)
                s = n - ATTN_FROM
                if 0 <= s < PAIRS:
                    exps(s)
                if 1 <= s < PAIRS + 1:
                    take_prob_t(s - 1)

            act.wait_ge(taken_dve, sum(m[0] not in BY_ACT for m in MIX_UNITS))
            squares(1)
            root(2)
            act.wait_ge(flipped, 2)
            act.copy(n_feat[:].rearrange("p (b c) s -> p b (c s)", b=4), ps[:, 2:6, :]).then_inc(feat_ready, 1)
            act.wait_ge(routed, 1)
            act.activation(logit_f[:], ps[0:EXPERTS, 0, 0:SEQ], ACT.Identity, bias=r_b[:, 0:1]).then_inc(logit_step, 1)
            act.wait_ge(route_step, 1)
            for t in range(TT):
                last = act.activation(weight[:, t, :], logit[:, t, :], ACT.Exp, bias=top0[:, t:t + 1])
            last.then_inc(logit_step, 1)
            act.wait_ge(routed, 4)
            act.copy(weight_t[:], ps[0:EXPERTS, 3, 0:SEQ]).then_inc(logit_step, 1)

            def start(r):
                g = r * (EXPERTS + 1) + 1
                act.wait_ge(gathered, g)
                act.copy(xg_sb, ps[:, XG, :]).then_inc(xg_ready, 1)
                act.wait_ge(xg_flipped, g)
                act.copy(xg_t, ps[:, XG_T, :].rearrange("p (c s) -> p c s", c=4)).then_inc(xg_t_ready, 1)

            def body(r, e):
                it = r * EXPERTS + e
                g = r * (EXPERTS + 1) + e + 1
                act.wait_ge(gate_ready, it + 1)
                act.activation(sig_sb, gate_sb, ACT.Sigmoid, scale=SWIGLU_ALPHA).then_inc(sig_ready, 1)
                act.wait_ge(gathered, g + 1)
                act.copy(xg_sb, ps[:, XG, :]).then_inc(xg_ready, 1)
                act.wait_ge(xg_flipped, g + 1)
                act.copy(xg_t, ps[:, XG_T, :].rearrange("p (c s) -> p c s", c=4)).then_inc(xg_t_ready, 1)
                act.wait_ge(act_flipped, it + 1)
                act.copy(act_t, ps[:, ACT_T, :].rearrange("p (c s) -> p c s", c=4)).then_inc(act_t_ready, 1)
                act.wait_ge(scat_flipped, it + 2)
                act.copy(scat_sb, ps[:, SCAT_T, 0:SEQ].rearrange("p (t s) -> p t s", t=TT)).then_inc(scat_ready, 1)
                act.wait_ge(unit_used, it * EXPERT_UNITS + (N_MIX + EXPERT_UNITS))
                act.copy(y_sb[:, 0, :], ps[:, Y0, :]).then_inc(y0_ready, 1)

            expert_passes(act, start, body, nothing)
            act.wait_ge(meaned, 3)
            act.activation(stat[:, 4:4 + TT], stat[:, 2:2 + TT], ACT.Sqrt).then_inc(rooted, 1)

        @block.vector
        def _(dve):
            done = [0]

            def link(ins):
                done[0] += 1
                ins.then_inc(dve_done, 1)
                dve.wait_ge(dve_done, done[0])

            def mean():
                link(dve.tensor_scalar(stat[:, 2:2 + TT], stat[:, 0:TT], 1.0 / D, EPS, ALU.mult, ALU.add))

            def inv_root(n):
                dve.wait_ge(rooted, n)
                link(dve.reciprocal(stat[:, 6:6 + TT], stat[:, 4:4 + TT]))

            def pairs(n):
                return ps[:, n % 2, :].rearrange("p (m s) -> p m s", m=2)

            def rope(n):
                name, i, _ = MIX_UNITS[n]
                dve.wait_ge(*taken(n))
                for t, name2 in ((z_raw, "cos"), (z_swap, "sin")):
                    last = dve.tensor_tensor(t[:], t[:], tb(name2).unsqueeze(1).to_broadcast([P, 2, SEQ]), ALU.mult)
                link(last)
                if name == "q":
                    dve.tensor_tensor(q_feat[:, 2 * i:2 * i + 2, :], z_raw[:], z_swap[:], ALU.add).then_inc(roped, 1)
                else:
                    for h in range(2):
                        rows = slice(h * HEAD_DIM, (h + 1) * HEAD_DIM)
                        last = dve.tensor_tensor(k_feat[rows, 2 * i:2 * i + 2, h, :], z_raw[rows], z_swap[rows],
                                                 ALU.add)
                    last.then_inc(roped, 1)

            def take(n):
                name, i, _ = MIX_UNITS[n]
                dve.wait_ge(unit_used, n + 1)
                two = slice(2 * i, 2 * i + 2)
                if name == "conv_x":
                    dve.wait_ge(*taken(4 * PER_GROUP - 1))
                    ins = dve.tensor_tensor(area_c[:, two, 2:SEQ + 2], pairs(n), conv[:, two, :], ALU.mult)
                    ins.then_inc(taken_dve, 1)
                    dve.wait_ge(*taken(n))
                    for m in range(2 * i, 2 * i + 2):
                        tmp = conv_tmp[:, m % 2, :]
                        link(dve.tensor_scalar(tmp, area_c[:, m, 2:SEQ + 2], taps[:, m, 2:3], None, ALU.mult))
                        for tap, dst in ((1, tmp), (0, conv[:, m, :])):
                            link(dve.scalar_tensor_tensor(out=dst, in0=area_c[:, m, tap:tap + SEQ],
                                                          scalar=taps[:, m, tap:tap + 1], in1=tmp,
                                                          op0=ALU.mult, op1=ALU.add))
                elif name == "conv_b":
                    dve.tensor_tensor(conv[:, two, :], pairs(n), conv[:, two, :], ALU.mult).then_inc(taken_dve, 1)
                elif name == "conv_out":
                    if i == 0:
                        dve.wait_ge(*taken(len(IN_UNITS) - 1))
                    dve.tensor_tensor(merged[:, two, :], pairs(n), gates[:, 0, two, :], ALU.mult).then_inc(taken_dve, 1)
                elif name == "attn_out":
                    link(dve.tensor_tensor(z_raw[:], pairs(n), gates[:, 1, two, :], ALU.mult))
                    dve.tensor_tensor(merged[:, two, :], merged[:, two, :], z_raw[:], ALU.add).then_inc(taken_dve, 1)
                    dve.wait_ge(*taken(n))
                else:
                    cols = slice(i * COLS, (i + 1) * COLS)
                    dve.tensor_tensor(h_tok[:, :, cols], h_tok[:, :, cols], pairs(n), ALU.add).then_inc(taken_dve, 1)

            def maxima(j):
                dve.wait_ge(scored, j + 1)
                for h in range(2):
                    diag = ps[:, 2 + h, :].rearrange("p (b s) -> p b s", b=2)[:, :, 0:P]
                    last = dve.tensor_tensor(diag, diag, tb("causal").unsqueeze(1).to_broadcast([P, 2, P]), ALU.add)
                link(last)
                for h in range(2):
                    dve.reduce_max(row_max[:, 2 * h:2 * h + 1], ps[:, 2 + h, 0:P], AX_X)
                    last = dve.reduce_max(row_max[:, 2 * h + 1:2 * h + 2], ps[:, 2 + h, P:3 * P], AX_X)
                link(last)
                dve.tensor_scalar(neg_max[:], row_max[:], -SCALE, None, ALU.mult).then_inc(max_ready, 1)

            def normalise(j):
                dve.wait_ge(exp_done, j + 1)
                link(dve.reciprocal(row_inv[:], row_sum[:]))
                for h in range(2):
                    for q in range(2):
                        i = 2 * h + q
                        lo, hi = (0, P) if q == 0 else (P, 3 * P)
                        last = dve.tensor_scalar(prob[:, h, lo:hi], prob[:, h, lo:hi], row_inv[:, i:i + 1], None,
                                                 ALU.mult)
                last.then_inc(prob_ready, 1)

            def take_attn(j):
                dve.wait_ge(attended, j + 1)
                dve.tensor_copy(q_feat[:, j, :], ps[:, 6, 0:SEQ]).then_inc(attn_taken, 1)

            dve.wait_ge(squared, TT)
            dve.tensor_scalar(stat[:, 2:2 + TT], stat[:, 0:TT], 1.0 / D, EPS, ALU.mult, ALU.add).then_inc(meaned, 1)
            inv_root(1)
            for t in range(TT):
                last = dve.tensor_scalar(n_tok[:, t, :], h_tok[:, t, :], stat[:, 6 + t:7 + t], None, ALU.mult)
            last.then_inc(normed, 1)
            dve.wait_ge(gain_in, 16)
            dve.wait_ge(flipped, 1)
            for c in range(KC):
                last = dve.tensor_scalar(n_feat[:, c, :], ps[:, 2 + c // 2, (c % 2) * SEQ:(c % 2 + 1) * SEQ],
                                         g_mix[:, c:c + 1], None, ALU.mult)
            last.then_inc(feat_ready, 1)
            dve.wait_ge(zeroed, 2)
            dve.wait_ge(small_in, 16 * 6)
            for n in range(N_MIX):
                if MIX_UNITS[n][0] in ("q", "k"):
                    rope(n)
                if MIX_UNITS[n][0] not in BY_ACT:
                    take(n)
                s = n - ATTN_FROM
                if 0 <= s < PAIRS:
                    maxima(s)
                    normalise(s)
                if 2 <= s < PAIRS + 2:
                    take_attn(s - 2)

            dve.wait_ge(squared, 2 * TT)
            dve.tensor_scalar(stat[:, 2:2 + TT], stat[:, 0:TT], 1.0 / D, EPS, ALU.mult, ALU.add).then_inc(meaned, 1)
            inv_root(2)
            for t in range(TT):
                last = dve.scalar_tensor_tensor(out=n_tok[:, t, :], in0=h_tok[:, t, :], scalar=stat[:, 6 + t:7 + t],
                                                in1=g_ffn[:], op0=ALU.mult, op1=ALU.mult)
            last.then_inc(normed, 1)
            dve.memset(y_sb[:, 0, :], 0.0).then_inc(y0_ready, 1)
            dve.memset(y_sb[:, 1, :], 0.0).then_inc(y1_ready, 1)
            dve.memset(scat_sb, 0.0).then_inc(scat_ready, 1)
            dve.memset(act_t, 0.0).then_inc(act_t_ready, 1)
            link(dve.memset(slot_of[:, :, EXPERTS:EXPERTS + 1], -1.0))
            dve.wait_ge(routed, 2)
            lg = ps[:, 1, 0:TT * EXPERTS].rearrange("p (t e) -> p t e", t=TT)
            dve.tensor_copy(logit[:], lg)
            link(dve.tensor_copy(left[:], lg))
            shape = [P, TT, EXPERTS]
            for k in range(TOP_K):
                m = top0 if k == 0 else top
                link(dve.tensor_reduce(m[:], left[:], AX_X, ALU.max))
                link(dve.tensor_tensor(hit[:], left[:], m[:].unsqueeze(2).to_broadcast(shape), ALU.is_equal))
                link(dve.tensor_tensor(hit[:], hit[:], tb("rank").unsqueeze(1).to_broadcast(shape), ALU.mult))
                link(dve.tensor_reduce(first[:], hit[:], AX_X, ALU.max))
                link(dve.tensor_tensor(hit[:], hit[:], first[:].unsqueeze(2).to_broadcast(shape), ALU.is_equal))
                if k == 0:
                    dve.tensor_copy(chosen[:], hit[:])
                else:
                    dve.tensor_tensor(chosen[:], chosen[:], hit[:], ALU.add)
                link(dve.scalar_tensor_tensor(out=left[:], in0=hit[:], scalar=MASKED, in1=left[:],
                                              op0=ALU.mult, op1=ALU.add))
            dve.tensor_scalar(top0[:], top0[:], -1.0, None, ALU.mult).then_inc(route_step, 1)
            dve.wait_ge(logit_step, 2)
            link(dve.tensor_tensor(weight[:], weight[:], chosen[:], ALU.mult))
            link(dve.tensor_reduce(top[:], weight[:], AX_X, ALU.add))
            link(dve.reciprocal(first[:], top[:]))
            dve.tensor_tensor(weight[:], weight[:], first[:].unsqueeze(2).to_broadcast(shape),
                              ALU.mult).then_inc(route_step, 1)
            dve.wait_ge(routed, 3)
            before = ps[:, 2, 0:TT * EXPERTS].rearrange("p (t e) -> p t e", t=TT)
            link(dve.scalar_tensor_tensor(out=slot_of[:, :, 0:EXPERTS], in0=before, scalar=1.0 + FIRST_SLOT,
                                          in1=chosen[:], op0=ALU.add, op1=ALU.mult))
            link(dve.tensor_scalar(slot_of[:, :, 0:EXPERTS], slot_of[:, :, 0:EXPERTS], -1.0, None, ALU.add))
            link(dve.tensor_reduce(most[:], ps[:, 2, TT * EXPERTS:(TT + 1) * EXPERTS], AX_X, ALU.max))
            dve.tensor_scalar(most_i[:], most[:], float(FIRST_SLOT), None, ALU.add).then_inc(route_step, 1)
            dve.wait_ge(route_step, ROUTE_STEPS)

            def next_tokens(e):
                for t in range(TT):
                    last = dve.tensor_scalar(onehot[:, t, :], tb("slot", 0, SLOTS), slot_of[:, t, bass.ds(e, 1)],
                                             None, ALU.is_equal)
                last.then_inc(onehot_ready, 1)

            def pick_bias(e):
                dve.tensor_copy(pick[:], tab[:, bass.ds(e + TABLE["ident"][0], 1)].to_broadcast([P, SLOTS])).then_inc(
                    pick_ready, 1)

            def start(r):
                if not isinstance(r, int):
                    dve.wait_ge(gathered, r * (EXPERTS + 1))
                    dve.wait_ge(scattered, r)
                    dve.memset(scat_sb, 0.0)
                    dve.tensor_scalar(slot_of[:], slot_of[:], -float(SLOTS), None, ALU.add).then_inc(route_step, 1)
                    dve.wait_ge(route_step, r + ROUTE_STEPS)
                next_tokens(0)
                pick_bias(0)

            def body(r, e):
                it = r * EXPERTS + e
                g = r * (EXPERTS + 1) + e + 1
                dve.wait_ge(gathered, g)
                next_tokens(e + 1)
                dve.wait_ge(scat_flipped, it + 1)
                for t in range(TT):
                    last = dve.tensor_scalar(whot[:, t, :], tb("slot"), slot_of[:, t, bass.ds(e, 1)],
                                             weight[:, t, bass.ds(e, 1)], ALU.is_equal, ALU.mult)
                last.then_inc(whot_ready, 1)
                dve.wait_ge(unit_used, it * EXPERT_UNITS + (N_MIX + GU_UNITS))
                dve.tensor_scalar(gate_sb, ps[:, GATE, :], SWIGLU_LIMIT, None, ALU.min).then_inc(gate_ready, 1)
                dve.tensor_scalar(up_sb, ps[:, UP, :], SWIGLU_LIMIT, -SWIGLU_LIMIT, ALU.min, ALU.max).then_inc(
                    up_ready, 1)
                pick_bias(e + 1)
                dve.wait_ge(gate_ready, it + 1)
                dve.wait_ge(up_ready, it * 2 + 1)
                dve.scalar_tensor_tensor(out=up_sb, in0=up_sb, scalar=1.0, in1=gate_sb, op0=ALU.add,
                                         op1=ALU.mult).then_inc(up_ready, 1)
                dve.wait_ge(up_ready, it * 2 + 2)
                dve.wait_ge(sig_ready, it + 1)
                dve.tensor_tensor(act_sb, up_sb, sig_sb, ALU.mult).then_inc(act_ready, 1)
                dve.wait_ge(unit_used, it * EXPERT_UNITS + (N_MIX + EXPERT_UNITS))
                dve.tensor_copy(y_sb[:, 1, :], ps[:, Y1, :]).then_inc(y1_ready, 1)

            def finish(r):
                dve.wait_ge(scattered, r + 1)

            expert_passes(dve, start, body, finish)

            for t in range(TT):
                for n in range(2):
                    cols = slice(n * HALF, (n + 1) * HALF)
                    link(dve.tensor_tensor(h_tok[:, t, cols], h_tok[:, t, cols], ps[:, 4 + 2 * t + n, :], ALU.add))
                link(dve.tensor_tensor(n_tok[:, t, :], h_tok[:, t, :], h_tok[:, t, :], ALU.mult))
                link(dve.tensor_reduce(stat[:, t:t + 1], n_tok[:, t, :], AX_X, ALU.add))
            dve.tensor_scalar(stat[:, 2:2 + TT], stat[:, 0:TT], 1.0 / D, EPS, ALU.mult, ALU.add).then_inc(meaned, 1)
            inv_root(3)
            for t in range(TT):
                dve.scalar_tensor_tensor(out=n_tok[:, t, :], in0=h_tok[:, t, :], scalar=stat[:, 6 + t:7 + t],
                                         in1=g_fin[:], op0=ALU.mult, op1=ALU.mult).then_inc(final_ready, 1)


def kernel(**inputs):
    import concourse.bacc as bacc
    from concourse.bass_utils import run_bass_kernel_spmd

    a = {n: np.ascontiguousarray(v) for n, v in inputs.items()}
    arrays = {
        "x": a["x"].reshape(SEQ, D),
        "table": constants(),
        "norm_mix_g": np.ascontiguousarray(a["norm_mix_g"].reshape(KC, P).T),
        "w_in": a["w_in"],
        "conv_w": np.ascontiguousarray(a["conv_w"].reshape(3, KC, P).transpose(2, 1, 0)),
        "w_conv_out": a["w_conv_out"],
        "w_attn_out": a["w_attn_out"],
        "w_out": a["w_out"],
        "norm_ffn_g": a["norm_ffn_g"],
        "router_w": a["router_w"],
        "router_b": a["router_b"].reshape(EXPERTS, 1),
        "w_gate_up": a["w_gate_up"],
        "b_gate_up": a["b_gate_up"],
        "w_down": a["w_down"],
        "b_down": a["b_down"],
        "norm_final_g": a["norm_final_g"],
    }
    nc = bacc.Bacc("TRN2", target_bir_lowering=False, num_devices=1)
    args = [nc.dram_tensor(f"in_{n}", v.shape, mybir.dt.from_np(v.dtype), kind="ExternalInput").ap()
            for n, v in arrays.items()]
    args.append(nc.dram_tensor("out_hidden", (SEQ, D), F32, kind="ExternalOutput").ap())
    build(nc, *args)
    r = run_bass_kernel_spmd(nc, [{f"in_{n}": v for n, v in arrays.items()}], core_ids=[0])
    return r.results[0]["out_hidden"].reshape(1, SEQ, D)
```

```python
from contextlib import ExitStack

import numpy as np

import concourse.bass as bass
from concourse import mybir

F32 = mybir.dt.float32
F32R = mybir.dt.float32r
I32 = mybir.dt.int32
ALU = mybir.AluOpType
ACT = mybir.ActivationFunctionType
AX_X = mybir.AxisListType.X

P = 128
D = 1024
SEQ = 256
HEADS = 16
HEAD_DIM = 64
EXPERTS = 32
TOP_K = 4
D_FF = 1024
EPS = 1e-5
SWIGLU_LIMIT = 7.0
SWIGLU_ALPHA = 1.702
ROPE_THETA = 10000.0
SCALE = HEAD_DIM ** -0.5

KC = D // P
TT = SEQ // P
HALF = 512
PAIRS = HEADS // 2
COLS = 256
UNIT = KC * COLS
RING = 8
AHEAD = 2
SLOTS = 64
FIRST_SLOT = 0
PASSES = (FIRST_SLOT + SEQ + SLOTS - 1) // SLOTS
MASKED = -3.0e38
BUSY_START, BUSY_LAST, BUSY_STEP, BUSY_TOP, BUSY_SLOTS = 24, 6, 3, 8, 4
ROUTE_STEPS = 2

GROUPS = [("q", 3 * D), ("k", 4 * D), ("v", 5 * D), ("conv_c", D), ("conv_x", 2 * D), ("conv_b", 0),
          ("gate_conv", 6 * D), ("gate_attn", 7 * D)]
PER_GROUP = D // COLS
IN_UNITS = [(g, i, c0 + i * COLS) for g, c0 in GROUPS for i in range(PER_GROUP)]
OUT_UNITS = [(g, i, i * COLS) for g in ("conv_out", "attn_out", "w_out") for i in range(PER_GROUP)]
MIX_UNITS = IN_UNITS + OUT_UNITS
N_MIX = len(MIX_UNITS)
ATTN_FROM = 3 * PER_GROUP
GU_UNITS = KC
DOWN_UNITS = KC // 2
EXPERT_UNITS = GU_UNITS + DOWN_UNITS
LATE = 8
LATE_ORDER = (6, 7, 0, 2, 1, 3, 4, 5)
LATE_FREE = (N_MIX - PER_GROUP,) * 2 + (N_MIX - 1,) * 2 + (N_MIX,) * 4
OWN = 3
FIRST_EXPERTS = 6
PAD = -3.4e38
TAKEN = 3.4e38
BY_ACT = ("q", "k", "v", "conv_c", "gate_conv", "gate_attn")

TABLE = {}
_at = 0
for _name, _n in (("ident", P), ("before", P), ("ones", P), ("causal", P), ("cos", SEQ), ("sin", SEQ),
                  ("slot", 2 * SLOTS)):
    TABLE[_name] = (_at, _at + _n)
    _at += _n
TABLE_COLS = _at


def constants():
    t = np.zeros((P, TABLE_COLS), np.float32)

    def put(name, a):
        lo, hi = TABLE[name]
        t[:, lo:hi] = a

    i = np.arange(P)
    put("ident", np.eye(P))
    put("before", i[:, None] < i[None, :])
    put("ones", 1.0)
    put("causal", np.where(i[None, :] <= i[:, None], 0.0, MASKED))
    half = HEAD_DIM // 2
    inv_freq = np.float32(ROPE_THETA) ** (-np.arange(half, dtype=np.float32) / np.float32(half))
    ang = np.arange(SEQ, dtype=np.float32)[None, :] * inv_freq.astype(np.float32)[i % half][:, None]
    put("cos", np.cos(ang))
    put("sin", np.where((i % HEAD_DIM < half)[:, None], -np.sin(ang), np.sin(ang)))
    put("slot", np.arange(2 * SLOTS) % SLOTS + 1)
    return t


def build(nc, x, table, norm_mix_g, w_in, conv_w, w_conv_out, w_attn_out, w_out, norm_ffn_g, router_w,
          router_b, w_gate_up, b_gate_up, w_down, b_down, norm_final_g, out):
    with ExitStack() as ctx:
        def sb(name, shape, dt=F32):
            return ctx.enter_context(nc.sbuf_tensor(name, shape, dt))

        def sem(name):
            return ctx.enter_context(nc.semaphore(name))

        ring = sb("ring", [P, RING, UNIT])
        with ExitStack() as mixing:
            def early(name, shape):
                return mixing.enter_context(nc.sbuf_tensor(name, shape, F32R))

            w_hi = early("w_hi", [P, AHEAD, UNIT])
            w_lo = early("w_lo", [P, AHEAD, UNIT])
            b_hi = early("b_hi", [P, KC, SEQ])
            b_lo = early("b_lo", [P, KC, SEQ])
            a_hi = early("a_hi", [P, KC, SEQ])
            a_lo = early("a_lo", [P, KC, SEQ])
        ring_late = sb("ring_late", [P, LATE, UNIT])
        tab = sb("tab", [P, TABLE_COLS])
        h_tok = sb("h_tok", [P, TT, D])
        n_tok = sb("n_tok", [P, TT, D])
        q_feat = sb("q_feat", [P, PAIRS, SEQ])
        area_a = sb("area_a", [P, 2 * KC * SEQ])
        area_b = sb("area_b", [P, KC * SEQ])
        area_c = sb("area_c", [P, KC, SEQ + 2])
        area_d = sb("area_d", [P, 4 * SEQ + 12 * P])
        g_ffn = sb("g_ffn", [P, D])
        g_fin = g_ffn
        g_mix = sb("g_mix", [P, KC])
        taps = sb("taps", [P, KC, 3])
        r_w = sb("r_w", [P, KC, EXPERTS])
        r_b = sb("r_b", [P, EXPERTS])
        stat = sb("stat", [P, 8])
        inv_h = sb("inv_h", [P, TT])
        spare = sb("spare", [P, 2])
        neg_max = sb("neg_max", [P, 4])
        row_max = sb("row_max", [P, 4])
        row_sum = sb("row_sum", [P, 4])
        row_inv = sb("row_inv", [P, 4])
        logit_f = sb("logit_f", [P, SEQ])
        logit = sb("logit", [P, TT, EXPERTS + 4])
        left = sb("left", [P, TT, EXPERTS + 4])
        top8 = sb("top8", [P, TT, 8])
        top = sb("top", [P, TT])
        top0 = sb("top0", [P, TT])
        first = sb("first", [P, TT])
        chosen = sb("chosen", [P, TT, EXPERTS])
        weight = sb("weight", [P, TT, EXPERTS])
        weight_t = sb("weight_t", [P, SEQ])
        part_sum = sb("part_sum", [P, TT, PER_GROUP])
        half_sum = sb("half_sum", [P, TT, 2])
        slot_of = sb("slot_of", [P, TT, EXPERTS + 1])
        most = sb("most", [P, 1])
        most_i = sb("most_i", [P, 1], I32)

        def tb(name, lo=0, n=None):
            a, b = TABLE[name]
            return tab[:, a + lo:(b if n is None else a + lo + n)]

        k_feat = area_a[:, :].rearrange("p (j h s) -> p j h s", j=PAIRS, h=2)
        gates = area_a[:, :].rearrange("p (g c s) -> p g c s", g=2, c=KC)
        conv = area_b[:, :].rearrange("p (c s) -> p c s", c=KC)
        merged = area_c[:, :, :].rearrange("p c s -> p (c s)")[:, 0:KC * SEQ].rearrange("p (c s) -> p c s", c=KC)
        z_raw, z_swap = (area_d[:, i * 2 * SEQ:(i + 1) * 2 * SEQ].rearrange("p (m s) -> p m s", m=2)
                         for i in range(2))
        prob, prob_t = (area_d[:, 4 * SEQ + i * 6 * P:4 * SEQ + (i + 1) * 6 * P].rearrange("p (h s) -> p h s", h=2)
                        for i in range(2))
        conv_tmp = z_raw
        n_feat = conv
        square = area_b[:, 0:D]

        def part(area, at, n):
            return area[:, at:at + n]

        gate_sb = part(area_a, 0, HALF)
        up_sb = part(area_a, HALF, HALF)
        sig_sb = part(area_a, 2 * HALF, HALF)
        act_sb = part(area_a, 3 * HALF, HALF)
        y_sb = part(area_a, 4 * HALF, 2 * HALF).rearrange("p (n c) -> p n c", n=2)
        scat_sb = part(area_a, 6 * HALF, SEQ).rearrange("p (t c) -> p t c", t=TT)
        final = part(area_a, 0, TT * D).rearrange("p (t c) -> p t c", t=TT)
        act_t = part(area_b, 0, HALF).rearrange("p (c s) -> p c s", c=4)
        xg_sb = part(area_b, HALF, HALF)
        xg_t = part(area_b, 2 * HALF, HALF).rearrange("p (c s) -> p c s", c=4)
        onehot = part(area_b, 3 * HALF, TT * SLOTS).rearrange("p (t s) -> p t s", t=TT)
        whot = part(area_b, 3 * HALF + TT * SLOTS, TT * P).rearrange("p (t s) -> p t s", t=TT)
        pick = part(area_a, 7 * HALF, 4 * SLOTS).rearrange("p (q s) -> p q s", q=4)
        b_gu = tb("cos", 0, 2 * SEQ)
        b_dn = part(area_a, 4 * HALF, D)

        ps = ctx.enter_context(nc.psum_tensor("ps", [P, 8, HALF], F32))
        GATE, UP, Y0, Y1 = 0, 1, 2, 3
        ACT_T, SCAT_T, XG, XG_T = GATE, UP, Y0, Y1
        LOGITS, LOGITS_T, COUNTS, SPARE_BANK = 7, 0, 1, 6

        ident_in = sem("ident_in")
        table_in = sem("table_in")
        x_in = [sem(f"x_in{t}") for t in range(TT)]
        gain_in = sem("gain_in")
        small_in = sem("small_in")
        bias_in = sem("bias_in")
        final_gain_in = sem("final_gain_in")
        slot_in = [sem(f"slot_in{i}") for i in range(RING)]
        unit_used = sem("unit_used")
        taken_act = sem("taken_act")
        taken_dve = sem("taken_dve")
        hi_done = sem("hi_done")
        lo_dve = sem("lo_dve")
        lo_pool = sem("lo_pool")
        hi_first = sem("hi_first")
        a_hi_ready = sem("a_hi_ready")
        x_lo_ready = sem("x_lo_ready")
        a_lo_ready = sem("a_lo_ready")
        b_hi_ready = sem("b_hi_ready")
        b_lo_ready = sem("b_lo_ready")
        own_in = [sem(f"own_in{i}") for i in range(OWN)]
        late_in = [sem(f"late_in{i}") for i in range(LATE)]
        zeroed = sem("zeroed")
        weight_zeroed = sem("weight_zeroed")
        hg_ready = sem("hg_ready")
        bias_zeroed = sem("bias_zeroed")
        ones_ready = sem("ones_ready")
        squared = sem("squared")
        squared_dve = sem("squared_dve")
        meaned = sem("meaned")
        rooted = sem("rooted")
        normed = sem("normed")
        x_flipped = sem("x_flipped")
        flipped = sem("flipped")
        feat_ready = sem("feat_ready")
        roped = sem("roped")
        scored = sem("scored")
        max_ready = sem("max_ready")
        exp_done = sem("exp_done")
        prob_ready = sem("prob_ready")
        prob_flipped = sem("prob_flipped")
        prob_t_ready = sem("prob_t_ready")
        attended = sem("attended")
        attn_taken = sem("attn_taken")
        routed = sem("routed")
        logit_step = sem("logit_step")
        route_step = sem("route_step")
        dve_done = sem("dve_done")
        onehot_ready = sem("onehot_ready")
        pick_ready = sem("pick_ready")
        whot_ready = sem("whot_ready")
        gathered = sem("gathered")
        xg_ready = sem("xg_ready")
        xg_flipped = sem("xg_flipped")
        xg_t_ready = sem("xg_t_ready")
        gate_ready = sem("gate_ready")
        up_ready = sem("up_ready")
        sig_ready = sem("sig_ready")
        act_ready = sem("act_ready")
        act_flipped = sem("act_flipped")
        act_t_ready = sem("act_t_ready")
        scat_flipped = sem("scat_flipped")
        scat_ready = sem("scat_ready")
        y0_ready = sem("y0_ready")
        y1_ready = sem("y1_ready")
        scattered = sem("scattered")
        summed = sem("summed")
        final_squared = sem("final_squared")
        final_meaned = sem("final_meaned")
        final_rooted = sem("final_rooted")
        final_summed = sem("final_summed")
        final_step = sem("final_step")
        weighted = sem("weighted")
        final_ready = sem("final_ready")
        stored = sem("stored")

        block = ctx.enter_context(nc.Block())

        def wait_unit(eng, n):
            eng.wait_ge(slot_in[n % RING], 16 * (n // RING + 1))

        own = (area_d[:, 0:UNIT], q_feat[:].rearrange("p c s -> p (c s)"),
               area_c[:].rearrange("p c s -> p (c s)")[:, 0:UNIT])

        def ring_place(n):
            return ring[:, n % RING, :], slot_in[n % RING], 16 * (n // RING + 1)

        def own_place(i, loads):
            return own[i], own_in[i], 16 * loads

        def late_place(i, loads):
            return ring_late[:, i, :], late_in[i], 16 * loads

        BUFFERS = RING + OWN + LATE

        def first_place(i):
            turn, at = divmod(i, BUFFERS)
            if at < RING:
                return ring_place(N_MIX + turn * RING + at)
            if at < RING + OWN:
                return own_place(at - RING, turn + 1)
            return late_place(LATE_ORDER[at - RING - OWN], turn + 1)

        FIRST_PLACES = [first_place(i) for i in range(FIRST_EXPERTS * EXPERT_UNITS)]

        def place(it, u):
            if isinstance(it, int) and it < FIRST_EXPERTS:
                return FIRST_PLACES[it * EXPERT_UNITS + u]
            buf, landed, value = FIRST_PLACES[(FIRST_EXPERTS - 1) * EXPERT_UNITS + u]
            return buf, landed, it * 16 + (value - 16 * (FIRST_EXPERTS - 1))

        def wait_expert_unit(eng, it, u):
            _, landed, value = place(it, u)
            eng.wait_ge(landed, value)

        def taken(n):
            by_act = MIX_UNITS[n][0] in BY_ACT
            count = sum((m[0] in BY_ACT) == by_act for m in MIX_UNITS[:n + 1])
            return (taken_act if by_act else taken_dve), count

        def expert_passes(eng, start, body, finish, begun=0, end=None):
            start(0)
            with eng.Fori(begun, EXPERTS) as e:
                body(0, e)
            finish(0)
            eng.wait_ge(route_step, ROUTE_STEPS)
            count = eng.value_load(most_i[0:1, 0:1], min_val=0, max_val=2 * SEQ)
            with eng.If(count > SLOTS):
                with eng.Fori(1, PASSES) as r:
                    start(r)
                    with eng.Fori(0, EXPERTS) as e:
                        body(r, e)
                    finish(r)
                if end is not None:
                    end()

        @block.sync
        def _(sp):
            mix_dram = {"conv_out": w_conv_out, "attn_out": w_attn_out, "w_out": w_out}

            def load_unit(n):
                name, _, c0 = MIX_UNITS[n]
                src = mix_dram.get(name, w_in)[:, c0:c0 + COLS].rearrange("(k p) n -> p k n", p=P)
                if n >= RING:
                    sp.wait_ge(lo_dve, n - RING + 1)
                    sp.wait_ge(lo_pool, n - RING + 1)
                sp.dma_start(ring[:, n % RING, :].rearrange("p (k n) -> p k n", k=KC), src).then_inc(
                    slot_in[n % RING], 16)

            for t in range(TT):
                sp.dma_start(h_tok[:, t, :], x[t * P:(t + 1) * P, :]).then_inc(x_in[t], 16)
            sp.dma_start(tb("ident"), table[:, 0:P]).then_inc(ident_in, 16)
            sp.dma_start(g_mix[:], norm_mix_g).then_inc(gain_in, 16)
            load_unit(0)
            sp.dma_start(tab[:, P:], table[:, P:]).then_inc(table_in, 16)
            load_unit(1)
            sp.dma_start(taps[:], conv_w).then_inc(small_in, 16)
            sp.dma_start(r_w[:], router_w.rearrange("(k p) e -> p k e", p=P)).then_inc(small_in, 16)
            sp.dma_start(r_b[:], router_b.partition_broadcast(P)).then_inc(small_in, 16)
            sp.dma_start(g_ffn[:], norm_ffn_g.partition_broadcast(P)).then_inc(small_in, 16)
            for n in range(2, N_MIX):
                if n == 3 * RING:
                    sp.wait_ge(roped, 2 * PER_GROUP)
                    for q in range(4):
                        sp.dma_start(b_gu[q * EXPERTS:(q + 1) * EXPERTS, :],
                                     b_gate_up[:, q * HALF:(q + 1) * HALF]).then_inc(bias_in, 16)
                load_unit(n)

            def load_expert_unit(it, e, u):
                buf, landed, _ = place(it, u)
                if u < GU_UNITS:
                    src = w_gate_up[bass.ds(e, 1), u * P:(u + 1) * P, :].rearrange("e p n -> (e p) n")
                else:
                    src = w_down[bass.ds(e, 1), :, :].rearrange(
                        "e (h c p) n -> c p (e h) n", h=2, c=DOWN_UNITS)[u - GU_UNITS]
                    buf = buf.rearrange("p (h n) -> p h n", h=2)
                sp.dma_start(buf, src).then_inc(landed, 16)

            def start(r):
                if not isinstance(r, int):
                    return
                def load_first(i):
                    load_expert_unit(i // EXPERT_UNITS, i // EXPERT_UNITS, i % EXPERT_UNITS)

                sp.wait_ge(attn_taken, PAIRS)
                load_first(RING)
                sp.wait_ge(a_hi_ready, KC + 1)
                sp.wait_ge(a_lo_ready, 1)
                load_first(RING + 1)
                def load_late(j):
                    sp.wait_ge(unit_used, LATE_FREE[j])
                    load_first(RING + OWN + j)

                for i in range(RING):
                    if i == RING - 2:
                        load_late(0)
                        load_late(1)
                    sp.wait_ge(lo_dve, N_MIX + i - RING + 1)
                    sp.wait_ge(lo_pool, N_MIX + i - RING + 1)
                    load_first(i)
                sp.wait_ge(bias_zeroed, 1)
                sp.dma_start(b_dn[0:EXPERTS, :], b_down).then_inc(bias_in, 16)
                sp.wait_ge(b_hi_ready, 8)
                sp.wait_ge(b_lo_ready, 8)
                load_first(RING + 2)
                for j in range(2, LATE):
                    load_late(j)
                sp.wait_ge(hg_ready, 4)
                sp.dma_start(g_fin[:], norm_final_g.partition_broadcast(P)).then_inc(final_gain_in, 16)
                for i in range(BUFFERS, FIRST_EXPERTS * EXPERT_UNITS):
                    sp.wait_ge(unit_used, N_MIX + i - BUFFERS + 1)
                    load_first(i)

            def body(r, e):
                it = r * EXPERTS + e
                for u in range(EXPERT_UNITS):
                    sp.wait_ge(unit_used, it * EXPERT_UNITS + (N_MIX + u + 1 - EXPERT_UNITS))
                    load_expert_unit(it, e, u)

            def finish(r):
                for q in range(2 * TT):
                    t, n = q // 2, q % 2
                    cols = slice(n * HALF, (n + 1) * HALF)
                    sp.wait_ge(final_ready, r * (2 * TT) + (q + 1))
                    sp.dma_start(out[t * P:(t + 1) * P, cols], final[:, t, cols]).then_inc(stored, 16)

            def end():
                sp.wait_ge(stored, PASSES * 2 * TT * 16)

            expert_passes(sp, start, body, finish, begun=FIRST_EXPERTS, end=end)
            sp.wait_ge(stored, 2 * TT * 16)

        @block.gpsimd
        def _(pool):
            def lo_half(n):
                pool.wait_ge(hi_done, n + 1)
                pool.tensor_tensor(w_lo[:, n % AHEAD, UNIT // 2:], ring[:, n % RING, UNIT // 2:],
                                   w_hi[:, n % AHEAD, UNIT // 2:].bitcast(F32), ALU.subtract).then_inc(lo_pool, 1)

            pool.memset(weight_t[:], 0.0).then_inc(weight_zeroed, 1)
            pool.memset(area_a[:], 0.0).then_inc(zeroed, 1)
            pool.memset(area_c[:, :, 0:2], 0.0).then_inc(zeroed, 1)
            pool.memset(logit[:, :, EXPERTS:], PAD).then_inc(zeroed, 1)
            lo_half(0)
            lo_half(1)
            for n in range(N_MIX):
                name, i, _ = MIX_UNITS[n]
                if n + AHEAD < N_MIX:
                    lo_half(n + AHEAD)
                if n == N_MIX - PER_GROUP:
                    pool.wait_ge(*taken(n - 1))
                    pool.memset(b_dn, 0.0).then_inc(bias_zeroed, 1)
                if name == "conv_b":
                    pool.wait_ge(b_hi_ready, i + 1)
                    two = slice(2 * i, 2 * i + 2)
                    pool.tensor_tensor(b_lo[:, two, :], conv[:, two, :], b_hi[:, two, :].bitcast(F32),
                                       ALU.subtract).then_inc(b_lo_ready, 1)
                if n == len(IN_UNITS) - 1:
                    pool.wait_ge(a_hi_ready, KC + 1)
                    pool.tensor_tensor(a_lo[:], q_feat[:], a_hi[:].bitcast(F32), ALU.subtract).then_inc(a_lo_ready, 1)

        @block.tensor
        def _(pe):
            def keep_busy(count, operand=tb("ident")):
                for _ in range(count):
                    pe.matmul(ps[:, SPARE_BANK, 0:P], operand, operand, start=True, stop=True)

            def flip_x(c):
                for t in range(TT):
                    mm = pe.transpose(ps[:, c, t * P:(t + 1) * P], n_tok[:, t, c * P:(c + 1) * P], tb("ident"))
                mm.then_inc(x_flipped, 1)

            def flip(i):
                for c in range(2 * i, 2 * i + 2):
                    for t in range(TT):
                        at = (c % 2) * SEQ + t * P
                        mm = pe.transpose(ps[:, 2 + c // 2, at:at + P], n_tok[:, t, c * P:(c + 1) * P], tb("ident"))
                mm.then_inc(flipped, 1)

            def part_logits(i):
                pe.wait_ge(feat_ready, i + 1)
                for k in range(2 * i, 2 * i + 2):
                    rows = slice((k % 4) * EXPERTS, (k % 4 + 1) * EXPERTS)
                    mm = pe.matmul(ps[rows, LOGITS, 0:SEQ], r_w[:, k, :], n_feat[:, k, :], start=(k < 4),
                                   stop=(k >= 4), skip_group_check=True)
                return mm

            def project(n):
                name, i, _ = MIX_UNITS[n]
                bank = n % 2
                w_parts = [w[:, n % AHEAD, :].rearrange("p (k n) -> p k n", k=KC) for w in (w_hi, w_lo)]
                x_parts = (b_hi, b_lo) if name in ("conv_out", "w_out") else (a_hi, a_lo)
                pe.wait_ge(lo_dve, n + 1)
                if n >= 2:
                    pe.wait_ge(*taken(n - 2))
                for k in range(KC):
                    if name == "w_out" and i == 0 and k % 2 == 0:
                        pe.wait_ge(b_lo_ready, 5 + k // 2)
                    if n == 0:
                        pe.wait_ge(x_lo_ready, k + 1)
                    if k == KC // 2:
                        pe.wait_ge(lo_pool, n + 1)
                    for m in range(2):
                        for wp, xp in ((0, 0), (0, 1), (1, 0)):
                            w, src = w_parts[wp], x_parts[xp]
                            if name in ("v", "w_out"):
                                left_op, right_op = src[:, k, m * P:(m + 1) * P], w[:, k, :]
                            else:
                                left_op, right_op = w[:, k, m * P:(m + 1) * P], src[:, k, :]
                            mm = pe.matmul(ps[:, bank, m * COLS:(m + 1) * COLS], left_op, right_op,
                                           start=(k + m + wp + xp == 0), stop=(k == KC - 1 and wp == 1),
                                           skip_group_check=True)
                mm.then_inc(unit_used, 1)

            def score(j):
                pe.wait_ge(roped, PER_GROUP + j // 2 + 1)
                if j >= 1:
                    pe.wait_ge(exp_done, j)
                pe.matmul(ps[:, 2, 0:SEQ].rearrange("p (h s) -> p h s", h=2), q_feat[:, j, 0:P],
                          k_feat[:, j, :, 0:P], start=True, stop=True)
                mm = pe.matmul(ps[:, 3, :].rearrange("p (h s) -> p h s", h=2), q_feat[:, j, P:SEQ],
                               k_feat[:, j, :, :], start=True, stop=True)
                mm.then_inc(scored, 1)

            def flip_prob(j):
                pe.wait_ge(prob_ready, j + 1)
                if j >= 1:
                    pe.wait_ge(prob_t_ready, j)
                for h in range(2):
                    for b in range(3):
                        mm = pe.transpose(ps[:, 4 + h, b * P:(b + 1) * P], prob[:, h, b * P:(b + 1) * P],
                                          tb("ident"))
                mm.then_inc(prob_flipped, 1)

            def attend(j):
                pe.wait_ge(prob_t_ready, j + 1)
                if j == 0:
                    pe.wait_ge(*taken(ATTN_FROM - 1))
                else:
                    pe.wait_ge(attn_taken, j)
                for kt in range(2):
                    for h in range(2):
                        v = n_tok[:, kt, j * P + h * HEAD_DIM:j * P + (h + 1) * HEAD_DIM]
                        lo = kt * P
                        mm = pe.matmul(ps[h * HEAD_DIM:(h + 1) * HEAD_DIM, 6, lo:SEQ], v,
                                       prob_t[:, h, 2 * lo:2 * lo + SEQ - lo], start=(kt == 0), stop=(kt == 1),
                                       skip_group_check=True)
                mm.then_inc(attended, 1)

            pe.wait_ge(weight_zeroed, 1)
            keep_busy(BUSY_START, weight_t[:, 0:P])
            pe.wait_ge(ident_in, 16)
            pe.wait_ge(normed, 1)
            for c in range(KC):
                flip_x(c)
            for n in range(N_MIX):
                if MIX_UNITS[n][0] == "attn_out" and MIX_UNITS[n][1] == 0:
                    pe.wait_ge(a_lo_ready, 1)
                if MIX_UNITS[n][0] == "conv_out" and MIX_UNITS[n][1] == 0:
                    pe.wait_ge(b_lo_ready, 4)
                project(n)
                if n == N_MIX - 1:
                    pe.wait_ge(small_in, 16 * 4)
                if MIX_UNITS[n][0] == "w_out" and MIX_UNITS[n][1] >= 1:
                    i = MIX_UNITS[n][1] - 1
                    if i >= 1:
                        part_logits(i - 1)
                    pe.wait_ge(hg_ready, i + 1)
                    flip(i)
                s = n - ATTN_FROM
                if 0 <= s < PAIRS:
                    score(s)
                if 1 <= s < PAIRS + 1:
                    flip_prob(s - 1)
                if 2 <= s < PAIRS + 2:
                    attend(s - 2)

            pe.wait_ge(table_in, 16)
            keep_busy(BUSY_LAST)
            part_logits(2)
            pe.wait_ge(hg_ready, 4)
            flip(3)
            keep_busy(BUSY_STEP)
            part_logits(3).then_inc(routed, 1)
            keep_busy(BUSY_STEP)
            pe.wait_ge(logit_step, 1)
            for t in range(TT):
                mm = pe.transpose(ps[:, LOGITS_T, t * P:(t + 1) * P], logit_f[:, t * P:(t + 1) * P], tb("ident"))
            mm.then_inc(routed, 1)
            keep_busy(BUSY_TOP)
            pe.wait_ge(route_step, 1)
            pe.matmul(ps[:, COUNTS, 0:TT * EXPERTS], tb("before"), chosen[:].rearrange("p t e -> p (t e)"),
                      start=True, stop=False)
            pe.matmul(ps[:, COUNTS, EXPERTS:TT * EXPERTS], tb("ones"), chosen[:, 0, :],
                      start=False, stop=True).then_inc(routed, 1)
            for t in range(TT):
                mm = pe.matmul(ps[:, LOGITS, 0:EXPERTS], tb("ones"), chosen[:, t, :],
                               start=(t == 0), stop=(t == TT - 1))
            mm.then_inc(routed, 1)
            keep_busy(BUSY_SLOTS)

            def flip_weights():
                pe.wait_ge(weighted, 1)
                for t in range(TT):
                    mm = pe.transpose(ps[0:EXPERTS, XG, t * P:(t + 1) * P], weight[:, t, :], tb("ident"))
                    if t == 0:
                        mm.then_inc(scat_flipped, 1)
                mm.then_inc(routed, 1)

            def start_result():
                for t in range(TT):
                    for n in range(2):
                        pe.matmul(ps[:, 4 + 2 * t + n, :], weight_t[:, t * P:(t + 1) * P],
                                  b_dn[:, n * HALF:(n + 1) * HALF], start=True, stop=True)

            def gather(g, busy):
                pe.wait_ge(onehot_ready, g)
                if not (isinstance(busy, int) and busy == 0):
                    pe.wait_ge(y0_ready, busy)
                for t in range(TT):
                    for n in range(2):
                        mm = pe.matmul(ps[n * SLOTS:(n + 1) * SLOTS, XG, :], onehot[:, t, :],
                                       n_tok[:, t, n * HALF:(n + 1) * HALF], start=(t == 0), stop=(t == TT - 1),
                                       skip_group_check=True)
                mm.then_inc(gathered, 1)

            def flip_gathered(g, busy):
                if isinstance(g, int) and g == 1:
                    keep_busy(BUSY_STEP)
                pe.wait_ge(xg_ready, g)
                if not (isinstance(busy, int) and busy == 0):
                    pe.wait_ge(y1_ready, busy)
                for c in range(4):
                    mm = pe.transpose(ps[:, XG_T, c * P:(c + 1) * P], xg_sb[:, c * P:(c + 1) * P], tb("ident"))
                mm.then_inc(xg_flipped, 1)

            def scatter(t, n, restart=False):
                return pe.matmul(ps[:, 4 + 2 * t + n, :], scat_sb[:, t, :], y_sb[:, n, :],
                                 start=restart, stop=True, skip_group_check=True)

            def start(r):
                g = r * (EXPERTS + 1) + 1
                gather(g, r * EXPERTS)
                flip_gathered(g, r * EXPERTS)
                if isinstance(r, int):
                    pe.wait_ge(bias_in, 16 * 5)
                    for e in range(FIRST_EXPERTS - 1):
                        if e == 0:
                            keep_busy(BUSY_STEP)
                        body(0, e)
                else:
                    for t in range(TT):
                        for n in range(2):
                            scatter(t, n, restart=True)

            def body(r, e):
                it = r * EXPERTS + e
                g = r * (EXPERTS + 1) + e + 1
                first_expert = isinstance(it, int) and it == 0
                pe.wait_ge(pick_ready, g)
                pe.wait_ge(act_t_ready, it + 1)
                if not (isinstance(it, int) and it == 0):
                    pe.wait_ge(scat_ready, it)
                for b in range(2):
                    for h in range(2):
                        pe.matmul(ps[h * SLOTS:(h + 1) * SLOTS, GATE + b, :], pick[:, 2 * b + h, :], b_gu,
                                  start=True, stop=False, skip_group_check=True)
                pe.wait_ge(xg_t_ready, g)
                for k in range(GU_UNITS):
                    wait_expert_unit(pe, it, k)
                    for b in range(2):
                        for h in range(2):
                            lo = b * D_FF + h * HALF
                            mm = pe.matmul(ps[h * SLOTS:(h + 1) * SLOTS, GATE + b, :],
                                           xg_t[:, k % 4, (k // 4) * SLOTS:(k // 4 + 1) * SLOTS],
                                           place(it, k)[0][:, lo:lo + HALF],
                                           start=False, stop=(k == GU_UNITS - 1), skip_group_check=True)
                    mm.then_inc(unit_used, 1)
                    if k == 0 and first_expert:
                        flip_weights()
                    if k == GU_UNITS // 2:
                        if first_expert:
                            pe.wait_ge(logit_step, 3)
                        gather(g + 1, it)
                flip_gathered(g + 1, it)
                if first_expert:
                    start_result()
                else:
                    scatter_waits(it)
                    for n in range(2):
                        scatter(0, n)
                pe.wait_ge(act_ready, it + 1)
                for c in range(4):
                    mm = pe.transpose(ps[:, ACT_T, c * P:(c + 1) * P], act_sb[:, c * P:(c + 1) * P], tb("ident"))
                mm.then_inc(act_flipped, 1)
                if not first_expert:
                    for n in range(2):
                        scatter(1, n)
                pe.wait_ge(whot_ready, it + 1)
                for t in range(TT):
                    mm = pe.transpose(ps[:, SCAT_T, t * P:(t + 1) * P], whot[:, t, :], tb("ident"))
                mm.then_inc(scat_flipped, 1)
                pe.wait_ge(act_t_ready, it + 2)
                pe.wait_ge(xg_t_ready, g + 1)
                for j in range(DOWN_UNITS):
                    wait_expert_unit(pe, it, GU_UNITS + j)
                    for n in range(2):
                        for h in range(2):
                            lo = h * D + n * HALF
                            mm = pe.matmul(ps[h * SLOTS:(h + 1) * SLOTS, Y0 + n, :],
                                           act_t[:, j, h * SLOTS:(h + 1) * SLOTS],
                                           place(it, GU_UNITS + j)[0][:, lo:lo + HALF],
                                           start=(j == 0), stop=(j == DOWN_UNITS - 1), skip_group_check=True)
                    mm.then_inc(unit_used, 1)

            def scatter_waits(n):
                pe.wait_ge(y0_ready, n)
                pe.wait_ge(y1_ready, n)
                pe.wait_ge(scat_ready, n)

            def finish(r):
                scatter_waits((r + 1) * EXPERTS)
                for t in range(TT):
                    for n in range(2):
                        scatter(t, n).then_inc(scattered, 1)

            expert_passes(pe, start, body, finish, begun=FIRST_EXPERTS - 1)

        @block.scalar
        def _(act):
            def load_root_table():
                act.wait_ge(ones_ready, 1)
                act.activation(spare[:, 1:2], spare[:, 0:1], ACT.Sqrt)

            def squares(t):
                act.activation(square, h_tok[:, t, :], ACT.Square,
                               accum_out=stat[:, t:t + 1]).then_inc(squared, 1)

            def hi(n):
                wait_unit(act, n)
                if n >= AHEAD:
                    act.wait_ge(unit_used, n - AHEAD + 1)
                act.copy(w_hi[:, n % AHEAD, :], ring[:, n % RING, :]).then_inc(hi_done, 1)

            def root(n):
                act.wait_ge(meaned, n)
                act.activation(stat[:, 4:4 + TT], stat[:, 2:2 + TT], ACT.Sqrt).then_inc(rooted, 1)

            def take(n):
                name, i, _ = MIX_UNITS[n]
                act.wait_ge(unit_used, n + 1)
                src = ps[:, n % 2, :].rearrange("p (m s) -> p m s", m=2)
                if name in ("q", "k"):
                    if n >= 1:
                        act.wait_ge(roped, n)
                    act.copy(z_raw, src)
                    for a in range(4):
                        b = a ^ 1
                        last = act.copy(z_swap[32 * a:32 * a + 32, :, :], src[32 * b:32 * b + 32, :, :])
                    last.then_inc(taken_act, 1)
                elif name == "v":
                    act.copy(n_tok[:, :, i * COLS:(i + 1) * COLS], src).then_inc(taken_act, 1)
                elif name == "conv_c":
                    act.copy(conv[:, 2 * i:2 * i + 2, :], src).then_inc(taken_act, 1)
                else:
                    g = ("gate_conv", "gate_attn").index(name)
                    act.activation(gates[:, g, 2 * i:2 * i + 2, :], src, ACT.Sigmoid).then_inc(taken_act, 1)

            def exps(j):
                act.wait_ge(max_ready, j + 1)
                if j >= 1:
                    act.wait_ge(prob_flipped, j)
                for q in range(2):
                    for h in range(2):
                        i = 2 * q + h
                        lo, n = (0, P) if q == 0 else (P, SEQ)
                        last = act.activation(prob[:, h, lo:lo + n], ps[:, 2 + q, h * n:(h + 1) * n], ACT.Exp,
                                              bias=neg_max[:, i:i + 1], scale=SCALE,
                                              accum_out=row_sum[:, i:i + 1])
                last.then_inc(exp_done, 1)

            def take_prob_t(j):
                act.wait_ge(prob_flipped, j + 1)
                if j >= 1:
                    act.wait_ge(attended, j)
                act.copy(prob_t, ps[:, 4:6, 0:3 * P]).then_inc(prob_t_ready, 1)

            load_root_table()
            act.wait_ge(x_in[0], 16)
            squares(0)
            root(1)
            act.wait_ge(gain_in, 16)
            wait_unit(act, 0)
            for half in range(2):
                cols = slice(half * (UNIT // 2), (half + 1) * (UNIT // 2))
                act.copy(w_hi[:, 0, cols], ring[:, 0, cols]).then_inc(hi_first if half == 0 else hi_done, 1)
            for c in range(KC):
                act.wait_ge(x_flipped, c + 1)
                act.activation(a_hi[:, c, :], ps[:, c, 0:SEQ], ACT.Copy,
                               scale=g_mix[:, c:c + 1]).then_inc(a_hi_ready, 1)
            hi(1)
            for n in range(N_MIX):
                name, i, _ = MIX_UNITS[n]
                two = slice(2 * i, 2 * i + 2)
                if n + AHEAD < N_MIX:
                    hi(n + AHEAD)
                if name in BY_ACT:
                    take(n)
                if name == "conv_b":
                    act.wait_ge(*taken(n))
                    act.copy(b_hi[:, two, :], conv[:, two, :]).then_inc(b_hi_ready, 1)
                if n == len(IN_UNITS) - 1:
                    act.wait_ge(attn_taken, PAIRS)
                    act.copy(a_hi[:], q_feat[:]).then_inc(a_hi_ready, 1)
                    load_root_table()
                if name == "attn_out":
                    act.wait_ge(*taken(n))
                    act.copy(b_hi[:, two, :], merged[:, two, :]).then_inc(b_hi_ready, 1)
                if name == "w_out" and i >= 1:
                    act.wait_ge(flipped, i)
                    act.copy(n_feat[:, 2 * i - 2:2 * i, :].rearrange("p c s -> p (c s)"),
                             ps[:, 1 + i, :]).then_inc(feat_ready, 1)
                if name == "w_out":
                    act.wait_ge(*taken(n))
                    for t in range(TT):
                        at = (i * TT + t) * COLS
                        act.activation(area_a[:, at:at + COLS], h_tok[:, t, i * COLS:(i + 1) * COLS], ACT.Square,
                                       accum_out=part_sum[:, t, i:i + 1]).then_inc(squared, 1)
                s = n - ATTN_FROM
                if 0 <= s < PAIRS:
                    exps(s)
                if 1 <= s < PAIRS + 1:
                    take_prob_t(s - 1)

            root(2)
            act.wait_ge(routed, 1)
            act.copy(logit_f[:], ps[:, LOGITS, 0:SEQ]).then_inc(logit_step, 1)
            act.wait_ge(route_step, 1)
            for t in range(TT):
                last = act.activation(weight[:, t, :], logit[:, t, 0:EXPERTS], ACT.Exp, bias=top0[:, t:t + 1])
            last.then_inc(logit_step, 1)
            def start(r):
                g = r * (EXPERTS + 1) + 1
                act.wait_ge(gathered, g)
                act.copy(xg_sb, ps[:, XG, :]).then_inc(xg_ready, 1)
                act.wait_ge(xg_flipped, g)
                act.copy(xg_t, ps[:, XG_T, :].rearrange("p (c s) -> p c s", c=4)).then_inc(xg_t_ready, 1)
                if isinstance(r, int):
                    act.wait_ge(routed, 5)
                    act.wait_ge(weight_zeroed, 1)
                    act.copy(weight_t[0:EXPERTS, :], ps[0:EXPERTS, XG, 0:SEQ]).then_inc(logit_step, 1)

            def body(r, e):
                it = r * EXPERTS + e
                g = r * (EXPERTS + 1) + e + 1
                act.wait_ge(gathered, g + 1)
                act.copy(xg_sb, ps[:, XG, :]).then_inc(xg_ready, 1)
                act.wait_ge(gate_ready, it + 1)
                act.activation(sig_sb, gate_sb, ACT.Sigmoid, scale=SWIGLU_ALPHA).then_inc(sig_ready, 1)
                act.wait_ge(xg_flipped, g + 1)
                act.copy(xg_t, ps[:, XG_T, :].rearrange("p (c s) -> p c s", c=4)).then_inc(xg_t_ready, 1)
                act.wait_ge(act_flipped, it + 1)
                act.copy(act_t, ps[:, ACT_T, :].rearrange("p (c s) -> p c s", c=4)).then_inc(act_t_ready, 1)
                act.wait_ge(scat_flipped, it + 2)
                act.copy(scat_sb, ps[:, SCAT_T, 0:SEQ].rearrange("p (t s) -> p t s", t=TT)).then_inc(scat_ready, 1)
                act.wait_ge(unit_used, it * EXPERT_UNITS + (N_MIX + EXPERT_UNITS))
                act.copy(y_sb[:, 0, :], ps[:, Y0, :]).then_inc(y0_ready, 1)

            def finish(r):
                load_root_table()
                for t in range(TT):
                    for n in range(2):
                        act.wait_ge(summed, r * (2 * TT) + (2 * t + n + 1))
                        cols = slice(n * HALF, (n + 1) * HALF)
                        act.activation(final[:, t, cols], h_tok[:, t, cols], ACT.Square,
                                       accum_out=half_sum[:, t, n:n + 1]).then_inc(final_squared, 1)
                    act.wait_ge(final_meaned, r * TT + (t + 1))
                    act.activation(stat[:, 4 + t:5 + t], stat[:, 2 + t:3 + t], ACT.Sqrt).then_inc(final_rooted, 1)

            expert_passes(act, start, body, finish)

        @block.vector
        def _(dve):
            done = [0]

            def link(ins):
                done[0] += 1
                ins.then_inc(dve_done, 1)
                dve.wait_ge(dve_done, done[0])

            def mean(src):
                dve.tensor_scalar(stat[:, 2:2 + TT], src, 1.0 / D, EPS, ALU.mult, ALU.add).then_inc(meaned, 1)

            def lo_half(n):
                dve.wait_ge(*((hi_first, 1) if n == 0 else (hi_done, n + 1)))
                dve.tensor_tensor(w_lo[:, n % AHEAD, 0:UNIT // 2], ring[:, n % RING, 0:UNIT // 2],
                                  w_hi[:, n % AHEAD, 0:UNIT // 2].bitcast(F32), ALU.subtract).then_inc(lo_dve, 1)

            def inv_root(n, to):
                dve.wait_ge(rooted, n)
                link(dve.reciprocal(to, stat[:, 4:4 + TT]))

            def pairs(n):
                return ps[:, n % 2, :].rearrange("p (m s) -> p m s", m=2)

            def rope(n):
                name, i, _ = MIX_UNITS[n]
                dve.wait_ge(*taken(n))
                for t, name2 in ((z_raw, "cos"), (z_swap, "sin")):
                    last = dve.tensor_tensor(t, t, tb(name2).unsqueeze(1).to_broadcast([P, 2, SEQ]), ALU.mult)
                link(last)
                if name == "q":
                    dve.tensor_tensor(q_feat[:, 2 * i:2 * i + 2, :], z_raw, z_swap, ALU.add).then_inc(roped, 1)
                else:
                    for h in range(2):
                        rows = slice(h * HEAD_DIM, (h + 1) * HEAD_DIM)
                        last = dve.tensor_tensor(k_feat[rows, 2 * i:2 * i + 2, h, :], z_raw[rows], z_swap[rows],
                                                 ALU.add)
                    last.then_inc(roped, 1)

            def take(n):
                name, i, _ = MIX_UNITS[n]
                dve.wait_ge(unit_used, n + 1)
                two = slice(2 * i, 2 * i + 2)
                if name == "conv_x":
                    dve.wait_ge(*taken(4 * PER_GROUP - 1))
                    ins = dve.tensor_tensor(area_c[:, two, 2:SEQ + 2], pairs(n), conv[:, two, :], ALU.mult)
                    ins.then_inc(taken_dve, 1)
                elif name == "conv_b":
                    dve.tensor_tensor(conv[:, two, :], pairs(n), conv[:, two, :], ALU.mult).then_inc(taken_dve, 1)
                elif name == "conv_out":
                    if i == 0:
                        dve.wait_ge(*taken(len(IN_UNITS) - 1))
                    dve.tensor_tensor(merged[:, two, :], pairs(n), gates[:, 0, two, :], ALU.mult).then_inc(taken_dve, 1)
                elif name == "attn_out":
                    link(dve.tensor_tensor(conv[:, two, :], pairs(n), gates[:, 1, two, :], ALU.mult))
                    dve.tensor_tensor(merged[:, two, :], merged[:, two, :], conv[:, two, :], ALU.add).then_inc(taken_dve, 1)
                else:
                    cols = slice(i * COLS, (i + 1) * COLS)
                    dve.tensor_tensor(h_tok[:, :, cols], h_tok[:, :, cols], pairs(n), ALU.add).then_inc(taken_dve, 1)

            def convolve(n):
                i = MIX_UNITS[n][1]
                dve.wait_ge(*taken(n))
                for step in range(3):
                    for m in range(2 * i, 2 * i + 2):
                        tap = 2 - step
                        tmp, src, gain = conv_tmp[:, m % 2, :], area_c[:, m, tap:tap + SEQ], taps[:, m, tap:tap + 1]
                        if step == 0:
                            last = dve.tensor_scalar(tmp, src, gain, None, ALU.mult)
                        else:
                            last = dve.scalar_tensor_tensor(out=tmp if step == 1 else conv[:, m, :], in0=src,
                                                            scalar=gain, in1=tmp, op0=ALU.mult, op1=ALU.add)
                    link(last)

            def maxima(j):
                dve.wait_ge(scored, j + 1)
                for q in range(2):
                    n = P * (q + 1)
                    diag = ps[:, 2 + q, 0:2 * n].rearrange("p (h s) -> p h s", h=2)[:, :, n - P:n]
                    last = dve.tensor_tensor(diag, diag, tb("causal").unsqueeze(1).to_broadcast([P, 2, P]), ALU.add)
                link(last)
                for q in range(2):
                    n = P * (q + 1)
                    last = dve.tensor_reduce(row_max[:, 2 * q:2 * q + 2],
                                             ps[:, 2 + q, 0:2 * n].rearrange("p (h s) -> p h s", h=2), AX_X, ALU.max)
                link(last)
                dve.tensor_scalar(neg_max[:], row_max[:], -SCALE, None, ALU.mult).then_inc(max_ready, 1)

            def normalise(j):
                dve.wait_ge(exp_done, j + 1)
                link(dve.reciprocal(row_inv[:], row_sum[:]))
                for q in range(2):
                    for h in range(2):
                        i = 2 * q + h
                        lo, hi = (0, P) if q == 0 else (P, 3 * P)
                        last = dve.tensor_scalar(prob[:, h, lo:hi], prob[:, h, lo:hi], row_inv[:, i:i + 1], None,
                                                 ALU.mult)
                last.then_inc(prob_ready, 1)

            def take_attn(j):
                dve.wait_ge(attended, j + 1)
                dve.tensor_copy(q_feat[:, j, :], ps[:, 6, 0:SEQ]).then_inc(attn_taken, 1)

            dve.memset(spare[:, 0:1], 1.0).then_inc(ones_ready, 1)
            dve.wait_ge(x_in[1], 16)
            dve.tensor_tensor_reduce(area_b[:, D:2 * D], h_tok[:, 1, :], h_tok[:, 1, :], 1.0, 0.0, ALU.mult,
                                     ALU.add, stat[:, 1:2]).then_inc(squared_dve, 1)
            dve.wait_ge(squared_dve, 1)
            dve.wait_ge(squared, 1)
            mean(stat[:, 0:TT])
            inv_root(1, stat[:, 6:6 + TT])
            for t in range(TT):
                last = dve.tensor_scalar(n_tok[:, t, :], h_tok[:, t, :], stat[:, 6 + t:7 + t], None, ALU.mult)
            last.then_inc(normed, 1)
            lo_half(0)
            dve.wait_ge(gain_in, 16)
            for c in range(KC):
                dve.wait_ge(a_hi_ready, c + 1)
                dve.scalar_tensor_tensor(out=a_lo[:, c, :], in0=ps[:, c, 0:SEQ], scalar=g_mix[:, c:c + 1],
                                         in1=a_hi[:, c, :].bitcast(F32), op0=ALU.mult,
                                         op1=ALU.subtract).then_inc(x_lo_ready, 1)
            lo_half(1)
            dve.wait_ge(zeroed, 2)
            dve.wait_ge(table_in, 16)
            dve.wait_ge(small_in, 16 * 4)
            for n in range(N_MIX):
                name, i, _ = MIX_UNITS[n]
                s = n - ATTN_FROM
                if name not in BY_ACT:
                    take(n)
                if 0 <= s < PAIRS:
                    maxima(s)
                if n + AHEAD < N_MIX:
                    lo_half(n + AHEAD)
                if name == "w_out":
                    dve.wait_ge(*taken(n))
                    cols = slice(i * COLS, (i + 1) * COLS)
                    dve.tensor_tensor(n_tok[:, :, cols], h_tok[:, :, cols],
                                      g_ffn[:, cols].unsqueeze(1).to_broadcast([P, TT, COLS]),
                                      ALU.mult).then_inc(hg_ready, 1)
                if name in ("q", "k"):
                    rope(n)
                if name == "conv_x":
                    convolve(n)
                if name == "attn_out":
                    two = slice(2 * i, 2 * i + 2)
                    dve.wait_ge(b_hi_ready, 5 + i)
                    dve.tensor_tensor(b_lo[:, two, :], merged[:, two, :], b_hi[:, two, :].bitcast(F32),
                                      ALU.subtract).then_inc(b_lo_ready, 1)
                if 0 <= s < PAIRS:
                    normalise(s)
                if 2 <= s < PAIRS + 2:
                    take_attn(s - 2)

            dve.wait_ge(flipped, 4)
            dve.wait_ge(feat_ready, 3)
            dve.tensor_copy(n_feat[:, KC - 2:, :].rearrange("p c s -> p (c s)"), ps[:, 5, :]).then_inc(feat_ready, 1)
            dve.wait_ge(squared, 1 + TT * PER_GROUP)
            link(dve.tensor_reduce(stat[:, 0:TT], part_sum[:], AX_X, ALU.add))
            mean(stat[:, 0:TT])
            inv_root(2, inv_h[:])
            dve.memset(slot_of[:, :, EXPERTS:EXPERTS + 1], 0.0).then_inc(act_t_ready, 1)
            dve.wait_ge(zeroed, 3)
            dve.wait_ge(routed, 2)
            link(dve.tensor_reduce(logit[:, :, 0:EXPERTS],
                                   ps[:, LOGITS_T, 0:SEQ].rearrange("p (t q e) -> p t e q", t=TT, q=4),
                                   AX_X, ALU.add))
            for t in range(TT):
                last = dve.scalar_tensor_tensor(out=logit[:, t, 0:EXPERTS], in0=logit[:, t, 0:EXPERTS],
                                                scalar=inv_h[:, t:t + 1], in1=r_b[:], op0=ALU.mult, op1=ALU.add)
            link(last)
            for t in range(TT):
                last = dve.max(top8[:, t, :], logit[:, t, 0:EXPERTS])
            link(last)
            dve.tensor_scalar(top0[:], top8[:, :, 0], -1.0, None, ALU.mult)
            link(dve.memset(top8[:, :, TOP_K:], PAD))
            for t in range(TT):
                last = dve.match_replace(left[:, t, :], top8[:, t, :], logit[:, t, :], TAKEN)
            link(last)
            dve.tensor_scalar(chosen[:], left[:, :, 0:EXPERTS], TAKEN, None, ALU.is_equal).then_inc(route_step, 1)
            dve.wait_ge(routed, 3)
            before = ps[:, COUNTS, 0:TT * EXPERTS].rearrange("p (t e) -> p t e", t=TT)
            link(dve.scalar_tensor_tensor(out=slot_of[:, :, 0:EXPERTS], in0=before, scalar=1.0 + FIRST_SLOT,
                                          in1=chosen[:], op0=ALU.add, op1=ALU.mult))

            def count_most():
                dve.wait_ge(routed, 4)
                link(dve.tensor_reduce(most[:], ps[:, LOGITS, 0:EXPERTS], AX_X, ALU.max))
                dve.tensor_scalar(most_i[:], most[:], float(FIRST_SLOT), None, ALU.add).then_inc(route_step, 1)
                dve.wait_ge(route_step, ROUTE_STEPS)

            def weigh():
                shape = [P, TT, EXPERTS]
                dve.wait_ge(logit_step, 2)
                link(dve.tensor_tensor(weight[:], weight[:], chosen[:], ALU.mult))
                link(dve.tensor_reduce(top[:], weight[:], AX_X, ALU.add))
                link(dve.reciprocal(first[:], top[:]))
                dve.tensor_tensor(weight[:], weight[:], first[:].unsqueeze(2).to_broadcast(shape),
                                  ALU.mult).then_inc(weighted, 1)
                dve.wait_ge(weighted, 1)

            def next_tokens(e):
                for t in range(TT):
                    last = dve.tensor_scalar(onehot[:, t, :], tb("slot", 0, SLOTS), slot_of[:, t, bass.ds(e, 1)],
                                             inv_h[:, t:t + 1], ALU.is_equal, ALU.mult)
                last.then_inc(onehot_ready, 1)

            def pick_bias(e):
                for q in range(4):
                    column = tab[:, bass.ds(e + (TABLE["ident"][0] + q * EXPERTS), 1)]
                    last = dve.tensor_copy(pick[:, q, :], column.to_broadcast([P, SLOTS]))
                last.then_inc(pick_ready, 1)

            def start(r):
                if not isinstance(r, int):
                    dve.wait_ge(gathered, r * (EXPERTS + 1))
                    dve.wait_ge(stored, r * (2 * TT * 16))
                    dve.wait_ge(scattered, r * (2 * TT))
                    dve.memset(scat_sb, 0.0)
                    dve.tensor_scalar(slot_of[:], slot_of[:], -float(SLOTS), None, ALU.add).then_inc(route_step, 1)
                    dve.wait_ge(route_step, r + ROUTE_STEPS)
                next_tokens(0)
                pick_bias(0)
                if isinstance(r, int):
                    count_most()
                    weigh()

            def body(r, e):
                it = r * EXPERTS + e
                g = r * (EXPERTS + 1) + e + 1
                dve.wait_ge(gathered, g)
                next_tokens(e + 1)
                dve.wait_ge(scat_flipped, it + 1)
                for t in range(TT):
                    last = dve.tensor_scalar(whot[:, t, :], tb("slot"), slot_of[:, t, bass.ds(e, 1)],
                                             weight[:, t, bass.ds(e, 1)], ALU.is_equal, ALU.mult)
                last.then_inc(whot_ready, 1)
                dve.wait_ge(unit_used, it * EXPERT_UNITS + (N_MIX + GU_UNITS))
                dve.tensor_scalar(gate_sb, ps[:, GATE, :], SWIGLU_LIMIT, None, ALU.min).then_inc(gate_ready, 1)
                dve.tensor_scalar(up_sb, ps[:, UP, :], SWIGLU_LIMIT, -SWIGLU_LIMIT, ALU.min, ALU.max).then_inc(
                    up_ready, 1)
                pick_bias(e + 1)
                dve.wait_ge(gate_ready, it + 1)
                dve.wait_ge(up_ready, it * 2 + 1)
                dve.scalar_tensor_tensor(out=up_sb, in0=up_sb, scalar=1.0, in1=gate_sb, op0=ALU.add,
                                         op1=ALU.mult).then_inc(up_ready, 1)
                dve.wait_ge(up_ready, it * 2 + 2)
                dve.wait_ge(sig_ready, it + 1)
                dve.tensor_tensor(act_sb, up_sb, sig_sb, ALU.mult).then_inc(act_ready, 1)
                dve.wait_ge(unit_used, it * EXPERT_UNITS + (N_MIX + EXPERT_UNITS))
                dve.tensor_copy(y_sb[:, 1, :], ps[:, Y1, :]).then_inc(y1_ready, 1)

            def finish(r):
                def add(t, n):
                    cols = slice(n * HALF, (n + 1) * HALF)
                    dve.wait_ge(scattered, r * (2 * TT) + (2 * t + n + 1))
                    dve.tensor_tensor(h_tok[:, t, cols], h_tok[:, t, cols], ps[:, 4 + 2 * t + n, :],
                                      ALU.add).then_inc(summed, 1)

                def final_mean(t):
                    dve.wait_ge(final_squared, r * (2 * TT) + 2 * (t + 1))
                    dve.tensor_tensor(stat[:, t:t + 1], half_sum[:, t, 0:1], half_sum[:, t, 1:2],
                                      ALU.add).then_inc(final_summed, 1)
                    dve.wait_ge(final_summed, r * TT + (t + 1))
                    dve.tensor_scalar(stat[:, 2 + t:3 + t], stat[:, t:t + 1], 1.0 / D, EPS, ALU.mult,
                                      ALU.add).then_inc(final_meaned, 1)

                def final_root(t):
                    dve.wait_ge(final_rooted, r * TT + (t + 1))
                    dve.reciprocal(stat[:, 6 + t:7 + t], stat[:, 4 + t:5 + t]).then_inc(final_step, 1)
                    dve.wait_ge(final_step, r * TT + (t + 1))

                def final_norm(t, n):
                    cols = slice(n * HALF, (n + 1) * HALF)
                    dve.scalar_tensor_tensor(out=final[:, t, cols], in0=h_tok[:, t, cols],
                                             scalar=stat[:, 6 + t:7 + t], in1=g_fin[:, cols], op0=ALU.mult,
                                             op1=ALU.mult).then_inc(final_ready, 1)

                add(0, 0)
                add(0, 1)
                add(1, 0)
                dve.wait_ge(final_gain_in, 16)
                final_mean(0)
                add(1, 1)
                dve.wait_ge(summed, (r + 1) * (2 * TT))
                final_root(0)
                final_norm(0, 0)
                final_mean(1)
                final_norm(0, 1)
                final_root(1)
                final_norm(1, 0)
                final_norm(1, 1)

            expert_passes(dve, start, body, finish)


def kernel(**inputs):
    import concourse.bacc as bacc
    from concourse.bass_utils import run_bass_kernel_spmd

    a = {n: np.ascontiguousarray(v) for n, v in inputs.items()}
    arrays = {
        "x": a["x"].reshape(SEQ, D),
        "table": constants(),
        "norm_mix_g": np.ascontiguousarray(a["norm_mix_g"].reshape(KC, P).T),
        "w_in": a["w_in"],
        "conv_w": np.ascontiguousarray(a["conv_w"].reshape(3, KC, P).transpose(2, 1, 0)),
        "w_conv_out": a["w_conv_out"],
        "w_attn_out": a["w_attn_out"],
        "w_out": a["w_out"],
        "norm_ffn_g": a["norm_ffn_g"],
        "router_w": a["router_w"],
        "router_b": a["router_b"],
        "w_gate_up": a["w_gate_up"],
        "b_gate_up": a["b_gate_up"],
        "w_down": a["w_down"],
        "b_down": a["b_down"],
        "norm_final_g": a["norm_final_g"],
    }
    nc = bacc.Bacc("TRN2", target_bir_lowering=False, num_devices=1)
    args = [nc.dram_tensor(f"in_{n}", v.shape, mybir.dt.from_np(v.dtype), kind="ExternalInput").ap()
            for n, v in arrays.items()]
    args.append(nc.dram_tensor("out_hidden", (SEQ, D), F32, kind="ExternalOutput").ap())
    build(nc, *args)
    r = run_bass_kernel_spmd(nc, [{f"in_{n}": v for n, v in arrays.items()}], core_ids=[0])
    return r.results[0]["out_hidden"].reshape(1, SEQ, D)
```
